# Optimizing a Trainium2 kernel written in Bass

```python
import math
import jax, jax.numpy as jnp
from jax import lax
import numpy as np

D_MODEL = 1024
BATCH = 1
SEQ = 256
DEPTH = 2

N_EVEN = (DEPTH + 1) // 2
N_ODD = DEPTH // 2
MIX_WIDTH = D_MODEL
HEAD_DIM = 64
GMLP_GROUPS = 4
GMLP_CHUNK = 128
GMLP_DIM = MIX_WIDTH // 2 // GMLP_GROUPS
GMLP_WIDTH = GMLP_GROUPS * GMLP_DIM
MOBA_HEADS = (MIX_WIDTH // 2) // HEAD_DIM
MOBA_WIDTH = MOBA_HEADS * HEAD_DIM
MOBA_BLOCK = 256
MOBA_TOPK = 3
MOBA_Q_BLOCK = 64
ROPE_THETA = 500000.0
ROPE_DIM = HEAD_DIM // 4
SB_HEADS = MIX_WIDTH // HEAD_DIM
SB_Q_BLOCK = 128
PEER_HEADS = 8
PEER_NKEYS = 128
PEER_NEXPERTS = PEER_NKEYS * PEER_NKEYS
PEER_DKEY = 256
PEER_TOPK = 16
PEER_TOKEN_CHUNK = 128
EVEN_IN = 2 * GMLP_WIDTH + 3 * MOBA_WIDTH
ODD_IN = 3 * SB_HEADS * HEAD_DIM
EPS = 1e-6

kernel_name = "hybrid_gmlp_moba_stickbreak_peer"

def rmsnorm(x, g):
    xf = x.astype(jnp.float32)
    y = xf * lax.rsqrt(jnp.mean(xf * xf, axis=-1, keepdims=True) + EPS)
    return (y * g.astype(jnp.float32)).astype(x.dtype)

def partial_rope(x, pos):
    half = ROPE_DIM // 2
    inv_freq = ROPE_THETA ** (-jnp.arange(half, dtype=jnp.float32) / half)
    ang = pos.astype(jnp.float32)[:, None] * inv_freq[None, :]
    cos = jnp.cos(ang)[None, :, None, :]
    sin = jnp.sin(ang)[None, :, None, :]
    xr = x[..., :ROPE_DIM].astype(jnp.float32)
    x1, x2 = xr[..., :half], xr[..., half:]
    rot = jnp.concatenate([x1 * cos - x2 * sin, x1 * sin + x2 * cos], axis=-1)
    return jnp.concatenate([rot.astype(x.dtype), x[..., ROPE_DIM:]], axis=-1)

def gmlp_spatial_gating(u, v, v_gain, w_s, b_s):
    B_, S_, G, Dg = u.shape
    u = jax.nn.gelu(u)
    v = rmsnorm(jax.nn.gelu(v), v_gain)
    n_chunks = S_ // GMLP_CHUNK
    vc = v.reshape(B_, n_chunks, GMLP_CHUNK, G, Dg)
    causal = jnp.tril(jnp.ones((GMLP_CHUNK, GMLP_CHUNK), dtype=bool))
    w = jnp.where(causal[None], w_s, 0.0).astype(v.dtype)
    mixed = jnp.einsum('gts,bcsgd->bctgd', w, vc) + b_s.T[None, None, :, :, None].astype(v.dtype)
    return u * mixed.reshape(B_, S_, G, Dg)

def moba_attention(q, k, v):
    B_, H, S_, Dh = q.shape
    scale = Dh ** -0.5
    nb = -(-S_ // MOBA_BLOCK)
    k_sel = min(MOBA_TOPK, nb)
    pad = nb * MOBA_BLOCK - S_
    kp = jnp.pad(k, ((0, 0), (0, 0), (0, pad), (0, 0)))
    vp = jnp.pad(v, ((0, 0), (0, 0), (0, pad), (0, 0)))
    kb = kp.reshape(B_, H, nb, MOBA_BLOCK, Dh)
    vb = vp.reshape(B_, H, nb, MOBA_BLOCK, Dh)
    kmean = jnp.mean(kb.astype(jnp.float32), axis=3)
    nq = S_ // MOBA_Q_BLOCK
    qc = q.reshape(B_, H, nq, MOBA_Q_BLOCK, Dh).transpose(2, 0, 1, 3, 4)
    bidx = jnp.arange(B_)[:, None, None, None]
    hidx = jnp.arange(H)[None, :, None, None]
    n_sel = k_sel * MOBA_BLOCK

    def one_block(args):
        ci, qi = args
        q_pos = ci * MOBA_Q_BLOCK + jnp.arange(MOBA_Q_BLOCK)
        own = (ci * MOBA_Q_BLOCK) // MOBA_BLOCK
        gate = jnp.einsum('bhqd,bhnd->bhqn', qi.astype(jnp.float32), kmean)
        gate = jnp.where(jnp.arange(nb) < own, gate, -jnp.inf)
        _, sel = lax.top_k(gate, k_sel)
        sel_valid = jnp.arange(k_sel) < own
        ks = kb[bidx, hidx, sel]
        vs = vb[bidx, hidx, sel]
        s_sel = jnp.einsum('bhqd,bhqnkd->bhqnk', qi, ks).astype(jnp.float32) * scale
        s_sel = jnp.where(sel_valid[:, None], s_sel, -jnp.inf).reshape(B_, H, MOBA_Q_BLOCK, n_sel)
        k_own = lax.dynamic_index_in_dim(kb, own, axis=2, keepdims=False)
        v_own = lax.dynamic_index_in_dim(vb, own, axis=2, keepdims=False)
        key_pos = own * MOBA_BLOCK + jnp.arange(MOBA_BLOCK)
        s_own = jnp.einsum('bhqd,bhkd->bhqk', qi, k_own).astype(jnp.float32) * scale
        s_own = jnp.where(key_pos[None, :] <= q_pos[:, None], s_own, -jnp.inf)
        p = jax.nn.softmax(jnp.concatenate([s_sel, s_own], axis=-1), axis=-1)
        p_sel = p[..., :n_sel].reshape(B_, H, MOBA_Q_BLOCK, k_sel, MOBA_BLOCK).astype(v.dtype)
        p_own = p[..., n_sel:].astype(v.dtype)
        return (jnp.einsum('bhqnk,bhqnkd->bhqd', p_sel, vs)
                + jnp.einsum('bhqk,bhkd->bhqd', p_own, v_own))

    out = lax.map(one_block, (jnp.arange(nq), qc))
    return out.transpose(1, 2, 0, 3, 4).reshape(B_, H, S_, Dh)

def stick_breaking_attention(q, k, v):
    B_, H, S_, Dh = q.shape
    scale = Dh ** -0.5
    nq = S_ // SB_Q_BLOCK
    qc = q.reshape(B_, H, nq, SB_Q_BLOCK, Dh).transpose(2, 0, 1, 3, 4)
    key_pos = jnp.arange(S_)

    def one_block(args):
        ci, qi = args
        q_pos = ci * SB_Q_BLOCK + jnp.arange(SB_Q_BLOCK)
        causal = key_pos[None, :] < q_pos[:, None]
        z = jnp.einsum('bhqd,bhkd->bhqk', qi, k).astype(jnp.float32) * scale
        log_beta = jax.nn.log_sigmoid(z)
        log_one_minus = jnp.where(causal, jax.nn.log_sigmoid(-z), 0.0)
        log_remaining = lax.cumsum(log_one_minus, axis=3, reverse=True) - log_one_minus
        a = jnp.where(causal, jnp.exp(log_beta + log_remaining), 0.0)
        return jnp.einsum('bhqk,bhkd->bhqd', a.astype(v.dtype), v)

    out = lax.map(one_block, (jnp.arange(nq), qc))
    return out.transpose(1, 2, 0, 3, 4).reshape(B_, H, S_, Dh)

def peer_ffn(h, w_q, subkeys, u_tab, v_tab):
    B_, S_, D = h.shape
    q = jnp.einsum('bsd,de->bse', h, w_q).reshape(B_, S_, PEER_HEADS, 2, PEER_DKEY // 2)
    s = jnp.einsum('bshpd,hpnd->bshpn', q, subkeys).astype(jnp.float32)
    s_top, i_top = lax.top_k(s, PEER_TOPK)
    cand = s_top[..., 0, :, None] + s_top[..., 1, None, :]
    cand_idx = i_top[..., 0, :, None] * PEER_NKEYS + i_top[..., 1, None, :]
    n_cand = PEER_TOPK * PEER_TOPK
    best, pos = lax.top_k(cand.reshape(B_, S_, PEER_HEADS, n_cand), PEER_TOPK)
    experts = jnp.take_along_axis(cand_idx.reshape(B_, S_, PEER_HEADS, n_cand), pos, axis=-1)
    gates = jax.nn.softmax(best, axis=-1).astype(h.dtype)
    n_tok = B_ * S_
    nt = n_tok // PEER_TOKEN_CHUNK
    hc = h.reshape(nt, PEER_TOKEN_CHUNK, D)
    ec = experts.reshape(nt, PEER_TOKEN_CHUNK, PEER_HEADS * PEER_TOPK)
    gc = gates.reshape(nt, PEER_TOKEN_CHUNK, PEER_HEADS * PEER_TOPK)

    def one_chunk(args):
        hi, ei, gi = args
        u = u_tab[ei]
        act = jax.nn.gelu(jnp.einsum('td,ted->te', hi, u))
        vv = v_tab[ei]
        return jnp.einsum('te,ted->td', gi * act, vv)

    out = lax.map(one_chunk, (hc, ec, gc))
    return out.reshape(B_, S_, D)

def setup_inputs(seed: int = 0) -> dict:
    key = jax.random.key(seed)
    ks = jax.random.split(key, 20)
    nrm = jax.random.normal
    f32 = jnp.float32
    D = D_MODEL
    return {
        "x": nrm(ks[0], (BATCH, SEQ, D), f32),
        "c": nrm(ks[1], (BATCH, D), f32),
        "w_mod": nrm(ks[2], (DEPTH, D, 6 * D), f32) * (0.5 * D ** -0.5),
        "b_mod": nrm(ks[3], (DEPTH, 6 * D), f32) * 0.02,
        "norm_mix": 1.0 + 0.02 * nrm(ks[4], (DEPTH, D), f32),
        "norm_ffn": 1.0 + 0.02 * nrm(ks[5], (DEPTH, D), f32),
        "even_w_in": nrm(ks[6], (N_EVEN, D, EVEN_IN), f32) * D ** -0.5,
        "gmlp_v_gain": 1.0 + 0.02 * nrm(ks[7], (N_EVEN, GMLP_GROUPS, GMLP_DIM), f32),
        "gmlp_w_s": nrm(ks[8], (N_EVEN, GMLP_GROUPS, GMLP_CHUNK, GMLP_CHUNK), f32) * GMLP_CHUNK ** -0.5,
        "gmlp_b_s": 1.0 + 0.02 * nrm(ks[9], (N_EVEN, GMLP_GROUPS, GMLP_CHUNK), f32),
        "moba_q_gain": 1.0 + 0.02 * nrm(ks[10], (N_EVEN, HEAD_DIM), f32),
        "moba_k_gain": 1.0 + 0.02 * nrm(ks[11], (N_EVEN, HEAD_DIM), f32),
        "even_w_out": nrm(ks[12], (N_EVEN, MIX_WIDTH, D), f32) * MIX_WIDTH ** -0.5,
        "odd_w_in": nrm(ks[13], (N_ODD, D, ODD_IN), f32) * D ** -0.5,
        "odd_w_out": nrm(ks[14], (N_ODD, MIX_WIDTH, D), f32) * MIX_WIDTH ** -0.5,
        "peer_w_q": nrm(ks[15], (DEPTH, D, PEER_HEADS * PEER_DKEY), f32) * D ** -0.5,
        "peer_subkeys": nrm(ks[16], (DEPTH, PEER_HEADS, 2, PEER_NKEYS, PEER_DKEY // 2), f32) * (PEER_DKEY // 2) ** -0.5,
        "peer_u": nrm(ks[17], (DEPTH, PEER_NEXPERTS, D), f32) * D ** -0.5,
        "peer_v": nrm(ks[18], (DEPTH, PEER_NEXPERTS, D), f32),
    }

def reference(x, c, w_mod, b_mod, norm_mix, norm_ffn, even_w_in, gmlp_v_gain, gmlp_w_s,
              gmlp_b_s, moba_q_gain, moba_k_gain, even_w_out, odd_w_in, odd_w_out,
              peer_w_q, peer_subkeys, peer_u, peer_v):
    B_, S_, D = x.shape
    pos = jnp.arange(S_)
    c_act = jax.nn.silu(c)
    split_even = [GMLP_WIDTH, 2 * GMLP_WIDTH, 2 * GMLP_WIDTH + MOBA_WIDTH,
                  2 * GMLP_WIDTH + 2 * MOBA_WIDTH]
    for layer in range(DEPTH):
        i = layer // 2
        mod = (c_act @ w_mod[layer] + b_mod[layer])[:, None, :]
        sh1, sc1, g1, sh2, sc2, g2 = jnp.split(mod, 6, axis=-1)
        h = rmsnorm(x, norm_mix[layer]) * (1.0 + sc1) + sh1
        if layer % 2 == 0:
            proj = h @ even_w_in[i]
            ua, va, qb, kb, vb = jnp.split(proj, split_even, axis=-1)
            ya = gmlp_spatial_gating(ua.reshape(B_, S_, GMLP_GROUPS, GMLP_DIM),
                                     va.reshape(B_, S_, GMLP_GROUPS, GMLP_DIM),
                                     gmlp_v_gain[i], gmlp_w_s[i], gmlp_b_s[i])
            q = partial_rope(rmsnorm(qb.reshape(B_, S_, MOBA_HEADS, HEAD_DIM), moba_q_gain[i]), pos)
            k = partial_rope(rmsnorm(kb.reshape(B_, S_, MOBA_HEADS, HEAD_DIM), moba_k_gain[i]), pos)
            v = vb.reshape(B_, S_, MOBA_HEADS, HEAD_DIM)
            yb = moba_attention(q.transpose(0, 2, 1, 3), k.transpose(0, 2, 1, 3), v.transpose(0, 2, 1, 3))
            y = jnp.concatenate([ya.reshape(B_, S_, GMLP_WIDTH),
                                 yb.transpose(0, 2, 1, 3).reshape(B_, S_, MOBA_WIDTH)], axis=-1) @ even_w_out[i]
        else:
            q, k, v = jnp.split(h @ odd_w_in[i], 3, axis=-1)
            q = q.reshape(B_, S_, SB_HEADS, HEAD_DIM).transpose(0, 2, 1, 3)
            k = k.reshape(B_, S_, SB_HEADS, HEAD_DIM).transpose(0, 2, 1, 3)
            v = v.reshape(B_, S_, SB_HEADS, HEAD_DIM).transpose(0, 2, 1, 3)
            ys = stick_breaking_attention(q, k, v)
            y = ys.transpose(0, 2, 1, 3).reshape(B_, S_, MIX_WIDTH) @ odd_w_out[i]
        x = x + g1 * y
        h = rmsnorm(x, norm_ffn[layer]) * (1.0 + sc2) + sh2
        x = x + g2 * peer_ffn(h, peer_w_q[layer], peer_subkeys[layer], peer_u[layer], peer_v[layer])
    return x


_drawn_inputs = setup_inputs


def setup_inputs(seed=0):
    import zlib

    import numpy as np

    out = dict(_drawn_inputs(seed))
    spreads = {}
    factors = {'gmlp_v_gain': 4.157, 'gmlp_b_s': 3.329, 'moba_q_gain': 5.358, 'moba_k_gain': 5.675}
    for name, (base, spread) in spreads.items():
        noise = np.random.default_rng([zlib.crc32(name.encode()), seed]).standard_normal(out[name].shape)
        drawn = base * np.exp(spread * noise) if base else spread * noise
        out[name] = __import__('jax').numpy.asarray(drawn.astype(out[name].dtype))
    for name, factor in factors.items():
        out[name] = (out[name] * factor).astype(out[name].dtype)
    return out
```

```python
from contextlib import ExitStack

import numpy as np

import concourse.bass as bass
from concourse import mybir

D, T, P = 1024, 256, 128
C = D // P
TT = T // P
HEADS, TOPK, NKEYS = 8, 16, 128
SLOTS = HEADS * TOPK
MODC = 6 * C
HALF = NKEYS // 2
GROUP = 4
EVEN_T, ODD_T, OUT_T, WQ_T = 20, 24, 8, 16
GM = 4
LAYERS = 2
ROPE_HALF, HEAD = 8, 64
EPS = 1e-6
NEG = -1e30
RAW, PAIRS = 4, MODC // 2


class Count:

    def __init__(self):
        self.n = 0

    def add(self, k=1):
        self.n += k
        return self.n


class Body:

    def __init__(self, eng, sem):
        self.eng, self.sem, self.n = eng, sem, 0

    def seq(self, ins):
        self.n += 1
        ins.then_inc(self.sem, 1)
        self.wait()

    def wait(self):
        self.eng.wait_ge(self.sem, self.n)

    def end(self):
        self.eng.sem_clear(self.sem)
        self.n = 0


class Tile:

    def __init__(self, first, dyn=0):
        self.st, self.dyn = first, dyn
        self.slot, self.pair = first % RAW, first % 2

    def count(self, k=0):
        return self.st + k + self.dyn

    def loaded(self):
        return 16 * (self.st // RAW + 1) + (16 // RAW) * self.dyn

    def has(self, k):
        return self.st >= k or not isinstance(self.dyn, int)


def program(nc, A, O):
    f32, f32r, u32 = mybir.dt.float32, mybir.dt.float32r, mybir.dt.uint32
    ALU, ACT, AX = mybir.AluOpType, mybir.ActivationFunctionType, mybir.AxisListType
    ctx = ExitStack()
    with ctx:
        def sb(name, shape, dt=f32):
            return ctx.enter_context(nc.sbuf_tensor(name, shape, dt))

        def sem(name):
            return ctx.enter_context(nc.semaphore(name))

        arena = sb("arena", [P, NKEYS * T])
        raw = sb("raw", [P, RAW, D])
        whi, wlo = sb("whi", [P, 2, D], f32r), sb("wlo", [P, 2, D], f32r)
        mhi, mlo = sb("mhi", [P, C, T], f32r), sb("mlo", [P, C, T], f32r)
        xT = sb("xT", [P, C, T])
        ghi, glo = sb("ghi", [P, 2, T], f32r), sb("glo", [P, 2, T], f32r)
        oneI = sb("oneI", [P, 2, GROUP, NKEYS], f32r)
        gJhi, gJlo = sb("gJhi", [P, 2, GROUP, HALF], f32r), sb("gJlo", [P, 2, GROUP, HALF], f32r)
        slotI = sb("slotI", [P, T])
        route = sb("route", [P, 3, T])
        slotI16 = sb("slotI16", [P, 16])
        route16 = sb("route16", [P, 3, 16])
        ident, ones, iota = sb("ident", [P, P]), sb("ones", [P, P]), sb("iota", [P, P])
        cact = sb("cact", [P, D])
        modv = sb("modv", [P, LAYERS, MODC])
        bmod = sb("bmod", [P, LAYERS, MODC])
        norms = sb("norms", [P, LAYERS, 2, C])
        modt = sb("modt", [P, MODC])
        modt8 = sb("modt8", [P, 8])
        gainA = sb("gainA", [P, C])
        small = sb("small", [P, 64])

        def carve(at):
            place = [at]

            def take(*shape, dt=f32):
                n = int(np.prod(shape))
                v = arena[:, place[0]:place[0] + n]
                place[0] += n
                assert place[0] <= NKEYS * T
                if dt != f32:
                    v = v.bitcast(dt)
                if len(shape) == 2:
                    v = v.rearrange("p (a b) -> p a b", a=shape[0])
                elif len(shape) == 3:
                    v = v.rearrange("p (a b c) -> p a b c", a=shape[0], b=shape[1])
                elif len(shape) == 4:
                    v = v.rearrange("p (a b c d) -> p a b c d", a=shape[0], b=shape[1], c=shape[2])
                return v
            return take, place

        low, _ = carve(0)
        modw = low(4, 2, D)
        junk = low(D)
        yT = low(C, T)
        uT, gv, vn = low(GM, T), low(TT, GM, P), low(TT, GM, P)
        wsT, bs, vg = low(GM, P), low(GM, P), low(GM, P)
        high, at_high = carve(NKEYS * T // 2)
        hf, sq = high(C, T), high(C, T)
        gsq = carve(NKEYS * T // 2)[0](TT * GM, P)
        vt, sd = high(T), high(T)
        qk_raw, qk, vbuf = high(2, 2, T), high(2, 2, T), high(2, TT, P)
        sqqk, rstd, qn, rot = high(2, T), high(2, T), high(2, T), high(2, T)
        st_, pr, aT = high(2, 384), high(2, 384), high(2, 384)
        blk64, rotM, ropeC, ropeS = high(P), high(P), high(T), high(T)
        negU, negones, maskKQ, maskQK, gmask = high(P), high(P), high(P), high(P), high(P)
        assert at_high[0] <= 30720
        subk = carve(30720)[0](2 * HEADS, P)
        AFTER_NORM = NKEYS * T // 2 + 2 * C * T + 2 * T
        scores = carve(AFTER_NORM)[0](HEADS, TT, 2, P)
        qT = carve(AFTER_NORM + 4096)[0](2 * HEADS, T)
        high, at_high = carve(AFTER_NORM + 4096)
        cur, cur2 = high(TT, 2, P), high(TT, 2, P)
        v16, i16 = high(TT, 2, TOPK), high(TT, 2, TOPK, dt=u32)
        cand, cand2 = high(TT, TOPK, TOPK), high(TT, TOPK, TOPK)
        best, pos = high(TT, TOPK), high(TT, TOPK, dt=u32)
        posA, posB = high(TT, TOPK, dt=u32), high(TT, TOPK, dt=u32)
        eq = high(TT, TOPK, TOPK)
        bestS, keyI, keyJ = high(TT, HEADS, TOPK), high(TT, HEADS, TOPK), high(TT, HEADS, TOPK)
        ssum = high(TT, HEADS)
        assert at_high[0] <= 30720
        ysb = carve(NKEYS * T // 2)[0](TT, D)

        bank = [ctx.enter_context(nc.psum_tensor(f"bank{b}", [P, 512], f32)) for b in range(8)]

        def stream_bank(t):
            return bank[4 + t.slot][:, 0:T]

        const_in, mix_in, subk_in = sem("const_in"), sem("mix_in"), sem("subk_in")
        raw_in = [sem(f"raw_in{s}") for s in range(RAW)]
        mod_in = [sem(f"mod_in{s}") for s in range(4)]
        mod_used = sem("mod_used")
        hi_done, lo_done, tile_done = sem("hi_done"), sem("lo_done"), sem("tile_done")
        act_evac = sem("act_evac")
        ghi_done, glo_done = sem("ghi_done"), sem("glo_done")
        oneI_done, gJ_done, w_done, w_used = sem("oneI_done"), sem("gJ_done"), sem("w_done"), sem("w_used")
        dve_own, act_own, pool_own = sem("dve_own"), sem("act_own"), sem("pool_own")
        dve_body = sem("dve_body")
        exp_c = sem("exp_c")
        sq_ready, ss_ready, var_ready, sd_ready = sem("sq_ready"), sem("ss_ready"), sem("var_ready"), sem("sd_ready")
        h_ready, mhi_ready, m_ready, x_ready = sem("h_ready"), sem("mhi_ready"), sem("m_ready"), sem("x_ready")
        gvar, gsd, vn_ready, mixed, ya_ready = (sem(n) for n in ("gvar", "gsd", "vn_ready", "mixed", "ya_ready"))
        qsq, qss, qvar, qsd, qn_ready, qrot, qk_ready = (sem(n) for n in (
            "qsq", "qss", "qvar", "qsd", "qn_ready", "qrot", "qk_ready"))
        z_ready, s_sub, s_exp, p_ready, pT_ready, a_ready, yp_ready, y_ready = (sem(n) for n in (
            "z_ready", "s_sub", "s_exp", "p_ready", "pT_ready", "a_ready", "yp_ready", "y_ready"))
        z_ln, sp_ready, cum_ready = sem("z_ln"), sem("sp_ready"), sem("cum_ready")
        sc_ready, sc_used, best_ready, bexp, gates_ready, routeT, route_ready = (sem(n) for n in (
            "sc_ready", "sc_used", "best_ready", "bexp", "gates_ready", "routeT", "route_ready"))
        y_copied, yT_ready, out_done = sem("y_copied"), sem("yT_ready"), sem("out_done")

        base, acts = [], []
        n = a = 0
        for l in range(LAYERS):
            b, ae = {}, {}
            for name, tiles, by in (("proj", EVEN_T if l == 0 else ODD_T, "a"), ("out", OUT_T, "d"),
                                    ("wq", WQ_T, "a"), ("u", NKEYS, "a"), ("v", NKEYS, "")):
                b[name], ae[name] = n, a
                n += tiles
                a += tiles if by == "a" else 0
            base.append(b)
            acts.append(ae)
        SRC = [{"proj": A["even_in"], "out": A["even_out"]}, {"proj": A["odd_in"], "out": A["odd_out"]}]

        block = ctx.enter_context(nc.Block())

        @block.sync
        def _(sp):
            def load(t, src):
                if t.has(RAW):
                    sp.wait_ge(lo_done, t.count(1 - RAW))
                sp.dma_start(raw[:, t.slot, :], src).then_inc(raw_in[t.slot], 16)

            def load_all(src, first, count, body=RAW):
                with sp.Fori(0, count // body) as i:
                    for s in range(body):
                        load(Tile(first + s, i * body), src[i * body + s])

            for dst, name in ((xT[:, :, :], "xT"), (norms[:, :, :, :], "norms"), (bmod[:, :, :], "bmod"),
                              (ident[:, :], "ident"), (ones[:, :], "ones"), (iota[:, :], "iota")):
                sp.dma_start(dst, A[name]).then_inc(const_in, 16)
            sp.dma_start(cact[:, :], A["c"].broadcast_to([P, D])).then_inc(const_in, 16)
            for l in range(LAYERS):
                b = base[l]
                proj, out = SRC[l]["proj"], SRC[l]["out"]
                for s in range(RAW):
                    load(Tile(b["proj"] + s), proj[s])
                if l:
                    sp.wait_ge(x_ready, 16)
                mix = [(maskKQ, "maskKQ"), (negU, "negU"), (negones, "negones")] if l else [
                    (vg.rearrange("p a b -> p (a b)"), "v_gain"), (bs.rearrange("p a b -> p (a b)"), "b_s"),
                    (wsT, "wsT"), (gmask, "gmask"), (blk64, "blk64"), (rotM, "rotM"), (ropeC, "ropeC"),
                    (ropeS, "ropeS"), (maskQK, "maskQK"), (small[:, 0:2], "qk_gain")]
                for dst, name in mix:
                    src = A[name].broadcast_to([P, GM * P]) if name in ("v_gain", "b_s") else A[name]
                    sp.dma_start(dst, src).then_inc(mix_in, 16)
                sp.dma_start(subk, A["subkeys"][l]).then_inc(subk_in, 16)
                for s in range(RAW, EVEN_T if l == 0 else ODD_T):
                    load(Tile(b["proj"] + s), proj[s])
                load_all(out, b["out"], OUT_T)
                load_all(A["w_q"][l], b["wq"], WQ_T)
                load_all(A["u"][l], b["u"], NKEYS)
                load_all(A["v"][l], b["v"], NKEYS)
            sp.wait_ge(x_ready, 32)
            sp.dma_start(O["y"], xT[:, :, :]).then_inc(out_done, 16)
            sp.wait_ge(out_done, 16)

        MIX0, MIX1 = 16 * 10, 16 * 13

        @block.gpsimd
        def _(pool):
            body = Body(pool, pool_own)

            def load_mod(l, q, dyn=0):
                total = l * PAIRS + q
                if total >= 4 or not isinstance(dyn, int):
                    pool.wait_ge(mod_used, 2 * (total - 3 + dyn))
                pool.dma_start(modw[:, total % 4, :, :], A["w_mod"][l, q + dyn]).then_inc(mod_in[total % 4], 16)

            for q in range(4):
                load_mod(0, q)
            with pool.Fori(1, PAIRS // 4) as i:
                for s in range(4):
                    load_mod(0, s, 4 * i)

            for l in range(LAYERS):
                pool.wait_ge(route_ready, l + 1)

                def onehots(g, dyn):
                    total = l * 128 + g
                    if total >= 2 or not isinstance(dyn, int):
                        pool.wait_ge(w_done, total - 1 + dyn)
                    body.seq(pool.tensor_tensor(
                        oneI[:, total % 2, :, :], iota[:, :].unsqueeze(1).broadcast_to([P, GROUP, NKEYS]),
                        slotI16[:, GROUP * (g % 4):GROUP * (g % 4) + GROUP].unsqueeze(2).broadcast_to(
                            [P, GROUP, NKEYS]), ALU.subtract))
                    pool.tensor_scalar(oneI[:, total % 2, :, :], oneI[:, total % 2, :, :].bitcast(f32), 0.0, None,
                                       ALU.is_equal).then_inc(oneI_done, 1)

                def keys16(i):
                    body.seq(pool.tensor_copy(slotI16[:, :], slotI[:, bass.ds(16 * i, 16)]))

                for half in range(2):
                    keys16(0)
                    for s in range(4):
                        onehots(64 * half + s, 0)
                    body.end()
                    with pool.Fori(1, 16) as i:
                        keys16(i)
                        for s in range(4):
                            onehots(64 * half + s, 4 * i)
                        body.end()
                if l == 0:
                    pool.wait_ge(tile_done, base[0]["v"] + HALF)
                    for q in range(4):
                        load_mod(1, q)
                    with pool.Fori(1, PAIRS // 4) as i:
                        for s in range(4):
                            load_mod(1, s, 4 * i)

        @block.scalar
        def _(act):
            own = Count()

            def hi(t):
                act.wait_ge(raw_in[t.slot], t.loaded())
                if t.has(2):
                    act.wait_ge(tile_done, t.count(-1))
                act.activation(whi[:, t.pair, :], raw[:, t.slot, :], ACT.Copy).then_inc(hi_done, 1)

            def evac(t, out, func=ACT.Copy, scale=1.0):
                act.wait_ge(tile_done, t.count(1))
                src = stream_bank(t)
                if len(out.shape) == 3:
                    src = src.rearrange("p (a b) -> p a b", a=TT)
                act.activation(out, src, func, scale=scale).then_inc(act_evac, 1)

            def norm(k):
                if k == 0:
                    act.wait_ge(const_in, 16 * 7)
                else:
                    act.wait_ge(x_ready, 8 * k)
                act.activation(sq, xT[:, :, :], ACT.Square).then_inc(sq_ready, 1)
                act.wait_ge(var_ready, k + 1)
                act.activation(sd, vt, ACT.Sqrt).then_inc(sd_ready, 1)
                for half in range(2):
                    act.wait_ge(h_ready, 2 * k + half + 1)
                    act.activation(mhi[:, 4 * half:4 * half + 4, :], hf[:, 4 * half:4 * half + 4, :],
                                   ACT.Copy).then_inc(mhi_ready, 1)

            act.wait_ge(const_in, 16 * 7)
            act.activation(junk, cact[:, :], ACT.Exp, scale=-1.0).then_inc(exp_c, 1)
            for l in range(LAYERS):
                b = base[l]
                norm(2 * l)
                pj = b["proj"]
                outs = []
                if l == 0:
                    outs += [(gv[:, :, g, :], ACT.Gelu_apprx_tanh, 1.0) for g in range(GM)]
                    outs += [(uT[:, g, :], ACT.Gelu_apprx_tanh, 1.0) for g in range(GM)]
                pairs = 4 if l == 0 else 8
                for p in range(pairs):
                    q_to = qk_raw if l == 0 else qk
                    outs += [(q_to[:, p % 2, 0, :], ACT.Copy, 0.125 if l else 1.0), (q_to[:, p % 2, 1, :], ACT.Copy, 1.0),
                             (vbuf[:, p % 2, :, :], ACT.Copy, 1.0)]
                first = len(outs) - 3 * pairs

                def step(s):
                    if s < len(outs):
                        hi(Tile(pj + s))
                    if 2 <= s < len(outs) + 2:
                        k = s - 2 - first
                        if k >= 6:
                            act.wait_ge(y_ready, 4 * l + k // 3 - 1)
                        evac(Tile(pj + s - 2), *outs[s - 2])

                for s in range(first + 3):
                    step(s)
                    if l == 0 and s == 6:
                        act.wait_ge(gvar, 1)
                        act.activation(small[:, 16:24], small[:, 8:16], ACT.Sqrt).then_inc(gsd, 1)
                for p in range(pairs):
                    s, e = first + 3 * p + 3, 4 * l + p + 1
                    step(s)
                    if l == 0:
                        act.wait_ge(act_evac, acts[0]["proj"] + s - 1)
                        act.activation(sqqk, qk_raw[:, p % 2, :, :], ACT.Square).then_inc(qsq, 1)
                        step(s + 1)
                        act.wait_ge(qvar, p + 1)
                        act.activation(rstd, sqqk, ACT.Sqrt).then_inc(qsd, 1)
                        step(s + 2)
                        act.wait_ge(s_sub, e)
                        act.activation(pr, st_, ACT.Exp, scale=0.125).then_inc(s_exp, 1)
                        for h in range(2):
                            act.wait_ge(pT_ready, 2 * p + h + 1)
                            act.activation(aT[:, h, :], bank[h][:, 0:384], ACT.Copy).then_inc(a_ready, 1)
                    else:
                        step(s + 1)
                        act.wait_ge(z_ready, e)
                        for h in range(2):
                            ins = act.activation(pr[:, h, :], bank[h][:, 0:384], ACT.Abs)
                        ins.then_inc(act_own, 1)
                        act.wait_ge(act_own, own.add())
                        act.activation(pr, pr, ACT.Exp, scale=-1.0).then_inc(act_own, 1)
                        act.wait_ge(act_own, own.add())
                        act.activation(pr, pr, ACT.Ln, bias=1.0).then_inc(z_ln, 1)
                        step(s + 2)
                        for h in range(2):
                            act.wait_ge(cum_ready, 2 * p + h + 1)
                            act.activation(aT[:, h, :], bank[h][:, 0:384], ACT.Exp).then_inc(a_ready, 1)
                    act.wait_ge(yp_ready, e)
                    c = (GM if l == 0 else 0) + p
                    act.activation(yT[:, c, :], bank[2][:, 0:T], ACT.Copy).then_inc(y_ready, 1)
                act.wait_ge(y_ready, 4 * l + pairs)
                if l == 0:
                    act.wait_ge(ya_ready, 1)
                act.activation(mhi[:, :, :], yT, ACT.Copy).then_inc(mhi_ready, 1)
                for s in range(OUT_T):
                    hi(Tile(b["out"] + s))
                norm(2 * l + 1)

                def wq(s, dyn, lag=True):
                    hi(Tile(b["wq"] + s, dyn))
                    if lag:
                        evac(Tile(b["wq"] + s - 2, dyn), qT[:, s - 2 + dyn, :])
                for s in range(4):
                    wq(s, 0, s >= 2)
                with act.Fori(1, WQ_T // 4) as i:
                    for s in range(4):
                        wq(s, 4 * i)
                for s in range(WQ_T - 2, WQ_T):
                    evac(Tile(b["wq"] + s), qT[:, s, :])
                for h in range(HEADS):
                    act.wait_ge(sc_ready, HEADS * l + h + 1)
                    act.activation(scores[:, h, :, :, :].rearrange("p a b c -> p (a b c)"), bank[h % 4][:, :],
                                   ACT.Copy).then_inc(sc_used, 1)

                def u_step(s, dyn, lag=True):
                    hi(Tile(b["u"] + s, dyn))
                    if lag:
                        evac(Tile(b["u"] + s - 2, dyn), arena[:, bass.ds((s - 2) * T + dyn * T, T)],
                             ACT.Gelu_apprx_tanh)
                for s in range(4):
                    u_step(s, 0, s >= 2)
                with act.Fori(1, HALF // 4) as i:
                    for s in range(4):
                        u_step(s, 4 * i)
                act.wait_ge(best_ready, l + 1)
                act.activation(bestS, bestS, ACT.Exp).then_inc(bexp, 1)
                with act.Fori(HALF // 4, NKEYS // 4) as i:
                    for s in range(4):
                        u_step(s, 4 * i)
                for s in range(NKEYS - 2, NKEYS):
                    evac(Tile(b["u"] + s), arena[:, s * T:(s + 1) * T], ACT.Gelu_apprx_tanh)

                for half in range(2):
                    with act.Fori(half * HALF // 4, (half + 1) * HALF // 4) as i:
                        for s in range(4):
                            t = Tile(b["v"] + s, 4 * i)
                            hi(t)
                            if s == 0:
                                act.wait_ge(w_used, 128 * l + 64 * (half + 1))
                            act.activation(ghi[:, t.pair, :], arena[:, bass.ds(s * T + i * (4 * T), T)],
                                           ACT.Copy).then_inc(ghi_done, 1)
                act.wait_ge(tile_done, b["v"] + NKEYS)
                for k in range(4):
                    act.activation(ysb[:, k // 2, 512 * (k % 2):512 * (k % 2) + 512], bank[4 + k][:, :],
                                   ACT.Copy).then_inc(y_copied, 1)

        @block.vector
        def _(dve):
            own = Count()

            def seq(ins):
                ins.then_inc(dve_own, 1)
                dve.wait_ge(dve_own, own.add())

            def lo(t):
                dve.wait_ge(hi_done, t.count(1))
                dve.tensor_tensor(wlo[:, t.pair, :], raw[:, t.slot, :], whi[:, t.pair, :].bitcast(f32),
                                  ALU.subtract).then_inc(lo_done, 1)

            def mod_pair(total, col, dyn=0):
                dve.wait_ge(mod_in[total % 4], 16 * (total // 4 + 1) + 4 * dyn)
                for r in range(2):
                    if total or r:
                        dve.wait_ge(mod_used, 2 * (total + dyn) + r)
                    dve.scalar_tensor_tensor(junk, modw[:, total % 4, r, :], 1.0, cact[:, :], ALU.mult, ALU.mult,
                                             accum_out=col[:, r:r + 1]).then_inc(mod_used, 1)

            def mod_add(l, a, b_, src):
                seq(dve.tensor_tensor(modv[:, l, a:b_], src[:, a:b_], bmod[:, l, a:b_], ALU.add))

            def norm(l, w):
                k = 2 * l + w
                sh, sc = 3 * C * w, 3 * C * w + C
                seq(dve.scalar_tensor_tensor(gainA[:, :], modv[:, l, sc:sc + C], 1.0, norms[:, l, w, :], ALU.add,
                                             ALU.mult))
                dve.wait_ge(ss_ready, k + 1)
                dve.tensor_scalar(vt, bank[2][:, 0:T], 1.0 / D, EPS, ALU.mult, ALU.add).then_inc(var_ready, 1)
                dve.wait_ge(sd_ready, k + 1)
                seq(dve.reciprocal(vt, sd))
                seq(dve.tensor_tensor(hf, xT[:, :, :], vt.unsqueeze(1).broadcast_to([P, C, T]), ALU.mult))
                for c in range(C):
                    ins = dve.tensor_scalar(hf[:, c, :], hf[:, c, :], gainA[:, c:c + 1],
                                            modv[:, l, sh + c:sh + c + 1], ALU.mult, ALU.add)
                    if c % 4 == 3:
                        ins.then_inc(h_ready, 1)
                for half in range(2):
                    cs = slice(4 * half, 4 * half + 4)
                    dve.wait_ge(mhi_ready, 5 * l + 3 * w + half + 1)
                    dve.tensor_tensor(mlo[:, cs, :], hf[:, cs, :], mhi[:, cs, :].bitcast(f32),
                                      ALU.subtract).then_inc(m_ready, 1)

            dve.wait_ge(exp_c, 1)
            seq(dve.tensor_scalar(junk, junk, 1.0, None, ALU.add))
            seq(dve.reciprocal(junk, junk))
            seq(dve.tensor_tensor(cact[:, :], cact[:, :], junk, ALU.mult))
            for q in range(8):
                mod_pair(q, modt[:, 2 * q:2 * q + 2])
            dve.wait_ge(mod_used, 16)
            mod_add(0, 0, 2 * C, modt)
            for l in range(LAYERS):
                b = base[l]
                norm(l, 0)
                pj = b["proj"]
                pairs = 4 if l == 0 else 8
                mods = list(range(8, PAIRS)) if l == 0 else []

                def step(s):
                    if s < (EVEN_T if l == 0 else ODD_T):
                        lo(Tile(pj + s))
                    if mods and s >= 2:
                        q = mods.pop(0)
                        mod_pair(q, modt[:, 2 * q:2 * q + 2])

                if l == 0:
                    dve.wait_ge(mix_in, MIX0)
                    seq(dve.tensor_tensor(wsT, wsT, gmask.unsqueeze(1).broadcast_to([P, GM, P]), ALU.mult))
                    for s in range(6):
                        step(s)
                    dve.wait_ge(act_evac, 4)
                    gvf = gv.rearrange("p a b c -> p (a b) c")
                    seq(dve.tensor_tensor(gsq, gvf, gvf, ALU.mult))
                    seq(dve.tensor_reduce(small[:, 8:16], gsq, AX.X, ALU.add))
                    dve.tensor_scalar(small[:, 8:16], small[:, 8:16], 1.0 / P, EPS, ALU.mult,
                                      ALU.add).then_inc(gvar, 1)
                    step(6)
                    step(7)
                    dve.wait_ge(gsd, 1)
                    seq(dve.reciprocal(small[:, 24:32], small[:, 16:24]))
                    seq(dve.tensor_tensor(vn.rearrange("p a b c -> p (a b) c"), gvf,
                                          small[:, 24:32].unsqueeze(2).broadcast_to([P, 8, P]), ALU.mult))
                    dve.tensor_tensor(vn, vn, vg.unsqueeze(1).broadcast_to([P, TT, GM, P]),
                                      ALU.mult).then_inc(vn_ready, 1)
                    step(8)
                    step(9)
                    dve.wait_ge(mixed, 1)
                    dve.wait_ge(act_evac, 8)
                    for g in range(GM):
                        m = bank[g // 2][:, T * (g % 2):T * (g % 2) + T].rearrange("p (a b) -> p a b", a=TT)
                        y = yT[:, g, :].rearrange("p (a b) -> p a b", a=TT)
                        seq(dve.tensor_tensor(y, m, bs[:, g, :].unsqueeze(1).broadcast_to([P, TT, P]), ALU.add))
                        ins = dve.tensor_tensor(yT[:, g, :], yT[:, g, :], uT[:, g, :], ALU.mult)
                    ins.then_inc(ya_ready, 1)
                    step(10)
                else:
                    for s in range(3):
                        step(s)
                first = 8 if l == 0 else 0
                for p in range(pairs):
                    s, e = first + 3 * p + 3, 4 * l + p + 1
                    step(s)
                    if l == 0:
                        dve.wait_ge(qss, p + 1)
                        dve.tensor_scalar(sqqk, bank[3][:, :].rearrange("p (a b) -> p a b", a=2), 1.0 / HEAD, EPS,
                                          ALU.mult, ALU.add).then_inc(qvar, 1)
                        step(s + 1)
                        dve.wait_ge(qsd, p + 1)
                        seq(dve.reciprocal(rstd, rstd))
                        for r in range(2):
                            ins = dve.scalar_tensor_tensor(qn[:, r, :], qk_raw[:, p % 2, r, :], small[:, r:r + 1],
                                                           rstd[:, r, :], ALU.mult, ALU.mult)
                        ins.then_inc(qn_ready, 1)
                        dve.wait_ge(qn_ready, p + 1)
                        seq(dve.tensor_tensor(qk[:, p % 2, :, :], qn, ropeC.unsqueeze(1).broadcast_to([P, 2, T]),
                                              ALU.mult))
                        dve.wait_ge(qrot, p + 1)
                        seq(dve.tensor_tensor(rot, bank[2][:, :].rearrange("p (a b) -> p a b", a=2),
                                              ropeS.unsqueeze(1).broadcast_to([P, 2, T]), ALU.mult))
                        dve.tensor_tensor(qk[:, p % 2, :, :], qk[:, p % 2, :, :], rot, ALU.add).then_inc(qk_ready, 1)
                        step(s + 2)
                        mx, rs = small[:, 32:36], small[:, 36:40]
                        SEG = ((0, P), (P, 384))
                        dve.wait_ge(z_ready, e)
                        for h in range(2):
                            for k, (f, g) in enumerate(SEG):
                                seq(dve.tensor_reduce(mx[:, 2 * h + k:2 * h + k + 1], bank[h][:, f:g], AX.X, ALU.max))
                        for h in range(2):
                            for k, (f, g) in enumerate(SEG):
                                ins = dve.tensor_scalar(st_[:, h, f:g], bank[h][:, f:g],
                                                        mx[:, 2 * h + k:2 * h + k + 1], None, ALU.subtract)
                        ins.then_inc(s_sub, 1)
                        dve.wait_ge(s_exp, e)
                        for k, (f, g) in enumerate(SEG):
                            seq(dve.tensor_reduce(rs[:, 2 * k:2 * k + 2], pr[:, :, f:g], AX.X, ALU.add))
                        seq(dve.reciprocal(rs, rs))
                        for h in range(2):
                            for k, (f, g) in enumerate(SEG):
                                ins = dve.tensor_scalar(pr[:, h, f:g], pr[:, h, f:g], rs[:, 2 * k + h:2 * k + h + 1],
                                                        None, ALU.mult)
                        ins.then_inc(p_ready, 1)
                    else:
                        step(s + 1)
                        dve.wait_ge(z_ln, p + 1)
                        for h in range(2):
                            dve.scalar_tensor_tensor(st_[:, h, :], bank[h][:, 0:384], 0.0, pr[:, h, :], ALU.max,
                                                     ALU.add).then_inc(sp_ready, 1)
                        step(s + 2)
                while mods:
                    step(99)
                if l == 0:
                    dve.wait_ge(mod_used, MODC)
                    mod_add(0, 2 * C, MODC, modt)
                dve.wait_ge(mhi_ready, 5 * l + 3)
                dve.tensor_tensor(mlo[:, :, :], yT, mhi[:, :, :].bitcast(f32), ALU.subtract).then_inc(m_ready, 1)
                for s in range(OUT_T + 2):
                    if s < OUT_T:
                        lo(Tile(b["out"] + s))
                    if s >= 2:
                        t, c = Tile(b["out"] + s - 2), s - 2
                        dve.wait_ge(tile_done, t.count(1))
                        dve.scalar_tensor_tensor(xT[:, c, :], stream_bank(t), modv[:, l, 2 * C + c:2 * C + c + 1],
                                                 xT[:, c, :], ALU.mult, ALU.add).then_inc(x_ready, 1)
                norm(l, 1)
                with dve.Fori(0, WQ_T // 4) as i:
                    for s in range(4):
                        lo(Tile(b["wq"] + s, 4 * i))

                body = Body(dve, dve_body)
                dve.wait_ge(sc_used, HEADS * (l + 1))
                with dve.Fori(0, HEADS) as i:
                    tiles = [Tile(b["u"] + s, 8 * i) for s in range(8)]
                    lo(tiles[0])
                    lo(tiles[1])
                    body.seq(dve.tensor_copy(cur, scores[:, bass.ds(i, 1), :, :, :].squeeze(1)))
                    for a in range(TT):
                        for q in range(2):
                            c1, c2, top, idx = cur[:, a, q, :], cur2[:, a, q, :], v16[:, a, q, :], i16[:, a, q, :]
                            body.seq(dve.max(top[:, 0:8], c1))
                            dve.max_index(idx[:, 0:8], top[:, 0:8], c1)
                            body.seq(dve.match_replace(c2, top[:, 0:8], c1, -3e38))
                            body.seq(dve.max(top[:, 8:16], c2))
                            body.seq(dve.max_index(idx[:, 8:16], top[:, 8:16], c2))
                            lo(tiles[2 + (2 * a + q)])
                    body.seq(dve.tensor_tensor(cand, v16[:, :, 0, :].unsqueeze(3).broadcast_to([P, TT, TOPK, TOPK]),
                                          v16[:, :, 1, :].unsqueeze(2).broadcast_to([P, TT, TOPK, TOPK]), ALU.add))
                    for a in range(TT):
                        c1 = cand[:, a, :, :].rearrange("p a b -> p (a b)")
                        c2 = cand2[:, a, :, :].rearrange("p a b -> p (a b)")
                        body.seq(dve.max(best[:, a, 0:8], c1))
                        dve.max_index(pos[:, a, 0:8], best[:, a, 0:8], c1)
                        body.seq(dve.match_replace(c2, best[:, a, 0:8], c1, -3e38))
                        body.seq(dve.max(best[:, a, 8:16], c2))
                        body.seq(dve.max_index(pos[:, a, 8:16], best[:, a, 8:16], c2))
                        lo(tiles[6 + a])
                    dve.tensor_scalar(posA, pos, 4, None, ALU.logical_shift_right)
                    body.seq(dve.tensor_scalar(posB, pos, TOPK - 1, None, ALU.bitwise_and))
                    for q, (at, key) in enumerate(((posA, keyI), (posB, keyJ))):
                        shape = [P, TT, TOPK, TOPK]
                        row = iota[:, 0:TOPK].unsqueeze(1).unsqueeze(1).broadcast_to(shape)
                        body.seq(dve.tensor_tensor(eq, row, at.unsqueeze(3).broadcast_to(shape), ALU.is_equal))
                        body.seq(dve.tensor_tensor(eq, eq, i16[:, :, q, :].unsqueeze(2).broadcast_to(shape), ALU.mult))
                        body.seq(dve.tensor_reduce(key[:, :, bass.ds(i, 1), :].squeeze(2), eq, AX.X, ALU.add))
                    body.seq(dve.tensor_copy(bestS[:, :, bass.ds(i, 1), :].squeeze(2), best))
                    body.end()
                bshape = [P, TT, HEADS, TOPK]
                seq(dve.tensor_copy(ssum, bestS[:, :, :, 0]))
                dve.tensor_tensor(bestS, bestS, ssum.unsqueeze(3).broadcast_to(bshape),
                                  ALU.subtract).then_inc(best_ready, 1)
                dve.wait_ge(bexp, l + 1)
                seq(dve.tensor_reduce(ssum, bestS, AX.X, ALU.add))
                seq(dve.reciprocal(ssum, ssum))
                dve.tensor_tensor(bestS, bestS, ssum.unsqueeze(3).broadcast_to(bshape),
                                  ALU.mult).then_inc(gates_ready, 1)
                dve.wait_ge(routeT, l + 1)
                dve.tensor_copy(route[:, 0, :], bank[2][:, T:2 * T])
                seq(dve.tensor_copy(route[:, 1, :].bitcast(f32r), bank[3][:, 0:T]))
                seq(dve.tensor_tensor(route[:, 2, :], bank[3][:, 0:T], route[:, 1, :], ALU.subtract))
                dve.tensor_copy(slotI[:, :], bank[2][:, 0:T]).then_inc(route_ready, 1)

                def gated(g, dyn, half):
                    total = l * 128 + 64 * half + g
                    if total >= 2 or not isinstance(dyn, int):
                        dve.wait_ge(w_done, total - 1 + dyn)
                    row = iota[:, HALF * half:HALF * half + HALF]
                    for k in range(GROUP):
                        col = 4 * (g % 4) + k
                        for part, dst in ((1, gJhi), (2, gJlo)):
                            ins = dve.tensor_scalar(dst[:, total % 2, k, :], row, route16[:, 0, col:col + 1],
                                                    route16[:, part, col:col + 1], ALU.is_equal, ALU.mult)
                    ins.then_inc(gJ_done, 1)

                def weigh(g, dyn, half):
                    total = l * 128 + 64 * half + g
                    dve.wait_ge(w_done, total + 1 + dyn)
                    t0 = g * GROUP + GROUP * dyn
                    part = arena[:, HALF * T * half:HALF * T * (half + 1)].rearrange("p (j t) -> p t j", t=T)
                    part = part[:, bass.ds(t0, GROUP), :]
                    w = bank[total % 2][:, 0:GROUP * HALF].rearrange("p (t j) -> p t j", t=GROUP)
                    dve.tensor_tensor(part, w, part, ALU.mult).then_inc(w_used, 1)

                def route_columns(s, dyn16):
                    if s == 0:
                        body.seq(dve.tensor_copy(route16[:, :, :], route[:, :, bass.ds(dyn16, 16)]))

                def body_b(dyn, i, first):
                    if l or not first:
                        dve.wait_ge(gJ_done, 128 * l + dyn)
                    for s in range(4):
                        lo(Tile(b["u"] + HALF + s, dyn))
                        route_columns(s, 16 * i)
                        gated(s, dyn, 0)
                        if first and s == 1:
                            dve.wait_ge(act_evac, acts[l]["u"] + HALF)
                        if not (first and s == 0):
                            weigh(s - 1, dyn, 0)
                    body.end()
                body_b(0, 0, True)
                with dve.Fori(1, 16) as i:
                    body_b(4 * i, i, False)

                def g_lo(t, j):
                    dve.wait_ge(ghi_done, j + 1)
                    dve.tensor_tensor(glo[:, t.pair, :], arena[:, bass.ds((j - 128 * l) * T, T)],
                                      ghi[:, t.pair, :].bitcast(f32), ALU.subtract).then_inc(glo_done, 1)

                def body_c(dyn, i, first):
                    dve.wait_ge(gJ_done, 128 * l + HALF + dyn)
                    for s in range(4):
                        t = Tile(b["v"] + s, dyn)
                        lo(t)
                        route_columns(s, 16 * i)
                        if first and s == 0:
                            weigh(63, 0, 0)
                        elif first and s == 1:
                            dve.wait_ge(act_evac, acts[l]["u"] + NKEYS)
                            weigh(0, 0, 1)
                        else:
                            weigh(s - 1, dyn, 1)
                        g_lo(t, 128 * l + s + dyn)
                        gated(s, dyn, 1)
                    body.end()
                body_c(0, 0, True)
                with dve.Fori(1, 16) as i:
                    body_c(4 * i, i, False)
                weigh(63, 0, 1)

                def body_d(dyn):
                    for s in range(8):
                        t = Tile(b["v"] + HALF + s, dyn)
                        lo(t)
                        g_lo(t, 128 * l + HALF + s + dyn)

                if l == 0:
                    with dve.Fori(0, PAIRS // 4) as i:
                        body_d(8 * i)
                        for q in range(4):
                            mod_pair(PAIRS + q, modt8[:, 2 * q:2 * q + 2], 4 * i)
                        dve.wait_ge(mod_used, MODC + 8 + 8 * i)
                        body.seq(dve.tensor_copy(modt[:, bass.ds(8 * i, 8)], modt8[:, :]))
                        body.end()
                    mod_add(1, 0, MODC, modt)
                    with dve.Fori(PAIRS // 4, HALF // 8) as i:
                        body_d(8 * i)
                else:
                    with dve.Fori(0, HALF // 8) as i:
                        body_d(8 * i)
                for c in range(C):
                    if c % 2 == 0:
                        dve.wait_ge(yT_ready, 4 * l + c // 2 + 1)
                    dve.scalar_tensor_tensor(xT[:, c, :], bank[c // 2][:, T * (c % 2):T * (c % 2) + T],
                                             modv[:, l, 5 * C + c:5 * C + c + 1], xT[:, c, :], ALU.mult,
                                             ALU.add).then_inc(x_ready, 1)

        @block.tensor
        def _(pe):
            def three(out, wh, wl, mh, ml, start=True, stop=True, swap=False):
                for k, (w, m) in enumerate(((wh, mh), (wh, ml), (wl, mh))):
                    ins = pe.matmul(out, w, m, start=start and k == 0, stop=stop and k == 2, skip_group_check=True)
                return ins

            def weights(t, swap=False):
                pe.wait_ge(lo_done, t.count(1))
                out = stream_bank(t)
                if swap:
                    for a in range(TT):
                        for c in range(C):
                            ws = slice(c * P, (c + 1) * P)
                            ms = slice(a * P, (a + 1) * P)
                            ins = three(out[:, a * P:(a + 1) * P], mhi[:, c, ms], mlo[:, c, ms],
                                        whi[:, t.pair, ws], wlo[:, t.pair, ws], c == 0, c == C - 1)
                else:
                    for c in range(C):
                        ws = slice(c * P, (c + 1) * P)
                        ins = three(out, whi[:, t.pair, ws], wlo[:, t.pair, ws], mhi[:, c, :], mlo[:, c, :],
                                    c == 0, c == C - 1)
                ins.then_inc(tile_done, 1)

            def norm(k):
                pe.wait_ge(sq_ready, k + 1)
                for c in range(C):
                    ins = pe.matmul(bank[2][:, 0:T], ones[:, :], sq[:, c, :], start=c == 0, stop=c == C - 1)
                ins.then_inc(ss_ready, 1)

            pe.wait_ge(const_in, 16 * 7)
            for l in range(LAYERS):
                b = base[l]
                norm(2 * l)
                pe.wait_ge(m_ready, 5 * l + 2)
                pj, ae = b["proj"], acts[l]["proj"]
                if l:
                    pe.wait_ge(y_copied, 4)
                tiles = EVEN_T if l == 0 else ODD_T
                first = 8 if l == 0 else 0
                pairs = 4 if l == 0 else 8

                def step(s):
                    if s >= tiles:
                        return
                    if s >= 4:
                        pe.wait_ge(act_evac, ae + s - 3)
                    weights(Tile(pj + s), swap=(l == 0 and s < GM) or (s >= first and (s - first) % 3 == 2))

                for s in range(first + 3):
                    step(s)
                    if l == 0 and s == 9:
                        pe.wait_ge(vn_ready, 1)
                        for g in range(GM):
                            for a in range(TT):
                                at = T * (g % 2) + a * P
                                ins = pe.matmul(bank[g // 2][:, at:at + P], vn[:, a, g, :], wsT[:, g, :],
                                                start=True, stop=True)
                        ins.then_inc(mixed, 1)
                pe.wait_ge(mix_in, MIX1 if l else MIX0)
                for p in range(pairs):
                    s, e = first + 3 * p + 3, 4 * l + p + 1
                    q, k, v = qk[:, p % 2, 0, :], qk[:, p % 2, 1, :], vbuf[:, p % 2, :, :]
                    heads = [slice(HEAD * h, HEAD * (h + 1)) for h in range(2)]
                    step(s)
                    if l == 0:
                        pe.wait_ge(qsq, p + 1)
                        if p:
                            pe.wait_ge(qvar, p)
                        for r in range(2):
                            ins = pe.matmul(bank[3][:, r * T:(r + 1) * T], blk64, sqqk[:, r, :],
                                            start=True, stop=True)
                        ins.then_inc(qss, 1)
                        step(s + 1)
                        pe.wait_ge(qn_ready, p + 1)
                        if p:
                            pe.wait_ge(y_ready, p)
                        for r in range(2):
                            ins = pe.matmul(bank[2][:, r * T:(r + 1) * T], rotM, qn[:, r, :], start=True, stop=True)
                        ins.then_inc(qrot, 1)
                        pe.wait_ge(qk_ready, p + 1)
                        if p == 0:
                            pe.wait_ge(ya_ready, 1)
                        else:
                            pe.wait_ge(a_ready, 2 * p)
                        for h, hd in enumerate(heads):
                            z = bank[h]
                            pe.matmul(z[:, 0:P], q[hd, 0:P], k[hd, 0:P], start=True, stop=False,
                                      skip_group_check=True)
                            pe.matmul(z[:, 0:P], ident[:, :], maskQK, start=False, stop=False,
                                      skip_group_check=True)
                            pe.matmul(z[:, P:384], q[hd, P:T], k[hd, :], start=False, stop=False,
                                      skip_group_check=True)
                            ins = pe.matmul(z[:, T:384], ident[:, :], maskQK, start=False, stop=True,
                                            skip_group_check=True)
                        ins.then_inc(z_ready, 1)
                        step(s + 2)
                        pe.wait_ge(p_ready, p + 1)
                        for h in range(2):
                            for r in range(3):
                                ins = pe.transpose(bank[h][:, r * P:(r + 1) * P], pr[:, h, r * P:(r + 1) * P],
                                                   ident[:, :])
                            ins.then_inc(pT_ready, 1)
                    else:
                        pe.wait_ge(act_evac, ae + s - 1)
                        pe.wait_ge(a_ready, 2 * (e - 1))
                        for h, hd in enumerate(heads):
                            z = bank[h]
                            pe.matmul(z[:, 0:T], k[hd, 0:P], q[hd, :], start=True, stop=False,
                                      skip_group_check=True)
                            pe.matmul(z[:, 0:P], ident[:, :], maskKQ, start=False, stop=False,
                                      skip_group_check=True)
                            pe.matmul(z[:, T:384], k[hd, P:T], q[hd, P:T], start=False, stop=False,
                                      skip_group_check=True)
                            ins = pe.matmul(z[:, T:384], ident[:, :], maskKQ, start=False, stop=True,
                                            skip_group_check=True)
                        ins.then_inc(z_ready, 1)
                        step(s + 1)
                        for h in range(2):
                            z, sp_ = bank[h], st_[:, h, :]
                            pe.wait_ge(sp_ready, 2 * p + h + 1)
                            pe.matmul(z[:, 0:T], negU, sp_[:, 0:T], start=False, stop=False, skip_group_check=True)
                            pe.matmul(z[:, P:T], negones, sp_[:, T:384], start=False, stop=False,
                                      skip_group_check=True)
                            pe.matmul(z[:, T:384], negU, sp_[:, T:384], start=False, stop=True,
                                      skip_group_check=True).then_inc(cum_ready, 1)
                        step(s + 2)
                    pe.wait_ge(y_ready, e - 1) if e > 1 else None
                    for h, hd in enumerate(heads):
                        pe.wait_ge(a_ready, 2 * (e - 1) + h + 1)
                        yo = bank[2]
                        pe.matmul(yo[hd, 0:T], v[:, 0, hd], aT[:, h, 0:T], start=True, stop=False,
                                  skip_group_check=True)
                        ins = pe.matmul(yo[hd, P:T], v[:, 1, hd], aT[:, h, T:384], start=False, stop=True,
                                        skip_group_check=True)
                    ins.then_inc(yp_ready, 1)

                pe.wait_ge(m_ready, 5 * l + 3)
                for s in range(OUT_T):
                    if s >= 4:
                        pe.wait_ge(x_ready, 16 * l + s - 3)
                    weights(Tile(b["out"] + s))
                norm(2 * l + 1)
                pe.wait_ge(m_ready, 5 * l + 5)

                def ring(name, s, dyn):
                    pe.wait_ge(act_evac, acts[l][name] + s - 3 + dyn)
                    weights(Tile(b[name] + s, dyn))

                with pe.Fori(0, WQ_T // 4) as i:
                    for s in range(4):
                        ring("wq", s, 4 * i)
                pe.wait_ge(act_evac, acts[l]["u"])
                pe.wait_ge(subk_in, 16 * (l + 1))
                for h in range(HEADS):
                    if h >= 4:
                        pe.wait_ge(sc_used, HEADS * l + h - 3)
                    for a in range(TT):
                        for q in range(2):
                            r = (2 * a + q) * P
                            ins = pe.matmul(bank[h % 4][:, r:r + P], qT[:, 2 * h + q, a * P:(a + 1) * P],
                                            subk[:, 2 * h + q, :], start=True, stop=True)
                    ins.then_inc(sc_ready, 1)
                with pe.Fori(0, HALF // 4) as i:
                    for s in range(4):
                        ring("u", s, 4 * i)
                pe.wait_ge(best_ready, l + 1)
                for a in range(TT):
                    for src, at in ((keyI, 0), (keyJ, T)):
                        pe.transpose(bank[2][:, at + a * P:at + (a + 1) * P],
                                     src[:, a, :, :].rearrange("p a b -> p (a b)"), ident[:, :])
                pe.wait_ge(gates_ready, l + 1)
                for a in range(TT):
                    ins = pe.transpose(bank[3][:, a * P:(a + 1) * P], bestS[:, a, :, :].rearrange("p a b -> p (a b)"),
                                       ident[:, :])
                ins.then_inc(routeT, 1)

                def onehot_product(g, dyn, half):
                    total = l * 128 + 64 * half + g
                    pe.wait_ge(oneI_done, total + 1 + dyn)
                    pe.wait_ge(gJ_done, total + 1 + dyn)
                    if total >= 2 or not isinstance(dyn, int):
                        pe.wait_ge(w_used, total - 1 + dyn)
                    for k in range(GROUP):
                        out = bank[total % 2][:, HALF * k:HALF * (k + 1)]
                        pe.matmul(out, oneI[:, total % 2, k, :], gJhi[:, total % 2, k, :], start=True, stop=False)
                        ins = pe.matmul(out, oneI[:, total % 2, k, :], gJlo[:, total % 2, k, :], start=False,
                                        stop=True)
                    ins.then_inc(w_done, 1)

                def body_b(dyn):
                    for s in range(4):
                        ring("u", HALF + s, dyn)
                        onehot_product(s, dyn, 0)
                body_b(0)
                with pe.Fori(1, 16) as i:
                    body_b(4 * i)

                def v_tile(s, dyn, start=False, stop=False):
                    t = Tile(b["v"] + s, dyn)
                    pe.wait_ge(lo_done, t.count(1))
                    pe.wait_ge(glo_done, 128 * l + s + 1 + dyn)
                    for a in range(TT):
                        ts_ = slice(a * P, (a + 1) * P)
                        for h in range(2):
                            vs = slice(512 * h, 512 * h + 512)
                            ins = three(bank[4 + 2 * a + h][:, :], ghi[:, t.pair, ts_], glo[:, t.pair, ts_],
                                        whi[:, t.pair, vs], wlo[:, t.pair, vs], start, stop)
                    return ins.then_inc(tile_done, 1)

                def body_c(dyn, start):
                    for s in range(4):
                        v_tile(s, dyn, start and s == 0)
                        onehot_product(s, dyn, 1)
                pe.wait_ge(act_evac, acts[l]["u"] + NKEYS)
                body_c(0, True)
                with pe.Fori(1, 16) as i:
                    body_c(4 * i, False)
                with pe.Fori(16, 31) as i:
                    for s in range(4):
                        v_tile(s, 4 * i)
                for s in range(4):
                    ins = v_tile(NKEYS - 4 + s, 0, False, s == 3)
                for c in range(C):
                    for a in range(TT):
                        if c == 0:
                            pe.wait_ge(y_copied, 4 * l + 2 * a + 1)
                            pe.wait_ge(w_used, 128 * (l + 1))
                        if c == 4:
                            pe.wait_ge(y_copied, 4 * l + 2 * a + 2)
                        at = T * (c % 2) + a * P
                        ins = pe.transpose(bank[c // 2][:, at:at + P], ysb[:, a, c * P:(c + 1) * P], ident[:, :])
                    if c % 2:
                        ins.then_inc(yT_ready, 1)


def constants():
    f = np.float32
    r = np.arange(P)
    q = r % HEAD
    ident = np.eye(P, dtype=f)
    inv = (500000.0 ** (-np.arange(ROPE_HALF, dtype=f) / ROPE_HALF)).astype(f)
    ang = np.arange(T, dtype=f)[None, :] * inv[q % ROPE_HALF][:, None]
    roped = (q < 2 * ROPE_HALF)[:, None]
    rot = np.zeros((P, P), f)
    for m in r:
        if q[m] < ROPE_HALF:
            rot[m + ROPE_HALF, m] = -1
        elif q[m] < 2 * ROPE_HALF:
            rot[m - ROPE_HALF, m] = 1
    return {
        "ident": ident, "ones": np.ones((P, P), f), "iota": np.tile(r.astype(f), (P, 1)),
        "blk64": (r[:, None] // HEAD == r[None, :] // HEAD).astype(f), "rotM": rot,
        "ropeC": np.where(roped, np.cos(ang), 1).astype(f), "ropeS": np.where(roped, np.sin(ang), 0).astype(f),
        "negU": -(r[:, None] >= r[None, :]).astype(f), "negones": -np.ones((P, P), f),
        "maskKQ": np.where(r[:, None] >= r[None, :], NEG, 0).astype(f),
        "maskQK": np.where(r[None, :] > r[:, None], NEG, 0).astype(f),
        "gmask": (r[:, None] <= r[None, :]).astype(f),
    }


def kernel(**inputs):
    import concourse.bacc as bacc
    from concourse.bass_utils import run_bass_kernel_spmd

    x = {k: np.asarray(v) for k, v in inputs.items()}
    pack = np.ascontiguousarray

    def tiles(w):
        return pack(w.reshape(C, P, -1, P).transpose(2, 1, 0, 3)).reshape(-1, P, D)

    def by_pair(w, starts, width):
        return [w[:, s + P * p:s + P * (p + 1)] for p in range(width // P) for s in starts]

    we, wo = x["even_w_in"][0], x["odd_w_in"][0]
    gw = GM * P
    even = np.concatenate([we[:, gw:2 * gw], we[:, 0:gw]] + by_pair(we, [2 * gw, 3 * gw, 4 * gw], gw), axis=1)
    odd = np.concatenate(by_pair(wo, [0, D, 2 * D], D), axis=1)
    gains = np.stack([np.concatenate([x[n][0]] * 2) for n in ("moba_q_gain", "moba_k_gain")], axis=1)
    data = {
        "xT": pack(x["x"][0].T.reshape(C, P, T).transpose(1, 0, 2)), "c": x["c"],
        "w_mod": pack(x["w_mod"].transpose(0, 2, 1).reshape(LAYERS, PAIRS, 2, P, D).transpose(0, 1, 3, 2, 4)),
        "bmod": pack(x["b_mod"].reshape(LAYERS, MODC, P).transpose(2, 0, 1)),
        "norms": pack(np.stack([x["norm_mix"], x["norm_ffn"]], 1).reshape(LAYERS, 2, C, P).transpose(3, 0, 1, 2)),
        "even_in": tiles(even), "even_out": tiles(x["even_w_out"][0]),
        "odd_in": tiles(odd), "odd_out": tiles(x["odd_w_out"][0]),
        "w_q": np.stack([tiles(w) for w in x["peer_w_q"]]),
        "subkeys": pack(x["peer_subkeys"].transpose(0, 4, 1, 2, 3)).reshape(LAYERS, P, 2 * HEADS, P),
        "u": np.stack([pack(u.reshape(P, P, C, P).transpose(1, 3, 2, 0)).reshape(NKEYS, P, D)
                       for u in x["peer_u"]]),
        "v": np.stack([pack(v.reshape(P, P, D).transpose(1, 0, 2)) for v in x["peer_v"]]),
        "v_gain": x["gmlp_v_gain"].reshape(1, gw), "b_s": x["gmlp_b_s"].reshape(1, gw),
        "wsT": pack(x["gmlp_w_s"][0].transpose(2, 0, 1)), "qk_gain": pack(gains),
    }
    data.update(constants())
    nc = bacc.Bacc("TRN2", target_bir_lowering=False, num_devices=1)
    A = {n: nc.dram_tensor(f"in_{n}", a.shape, mybir.dt.float32, kind="ExternalInput").ap() for n, a in data.items()}
    O = {"y": nc.dram_tensor("out_y", (P, C, T), mybir.dt.float32, kind="ExternalOutput").ap()}
    program(nc, A, O)
    r = run_bass_kernel_spmd(nc, [{f"in_{n}": a for n, a in data.items()}], core_ids=[0])
    y = r.results[0]["out_y"]
    return pack(y.transpose(2, 1, 0)).reshape(1, T, D)
```

```python
from contextlib import ExitStack

import numpy as np

import concourse.bass as bass
from concourse import mybir

D, T, P = 1024, 256, 128
C = D // P
TT = T // P
HEADS, TOPK, NKEYS = 8, 16, 128
SLOTS = HEADS * TOPK
MODC = 6 * C
HALF = NKEYS // 2
GROUP, STEP = 4, 8
STEPS = T // STEP
EVEN_T, ODD_T, OUT_T, WQ_T = 20, 24, 8, 16
GM = 4
LAYERS = 2
ROPE_HALF, HEAD = 8, 64
EPS = 1e-6
NEG = -1e30
RAW, PAIRS = 4, MODC // 2


class Count:

    def __init__(self):
        self.n = 0

    def add(self, k=1):
        self.n += k
        return self.n


class Body:

    def __init__(self, eng, sem):
        self.eng, self.sem, self.n = eng, sem, 0

    def seq(self, ins):
        self.n += 1
        ins.then_inc(self.sem, 1)
        self.wait()

    def go(self, ins):
        self.n += 1
        ins.then_inc(self.sem, 1)

    def wait(self, back=0):
        self.eng.wait_ge(self.sem, self.n - back)

    def end(self):
        self.eng.sem_clear(self.sem)
        self.n = 0


class Tile:

    def __init__(self, first, dyn=0):
        self.st, self.dyn = first, dyn
        self.slot, self.pair = first % RAW, first % 2

    def count(self, k=0):
        return self.st + k + self.dyn

    def loaded(self):
        return 16 * (self.st // RAW + 1) + (16 // RAW) * self.dyn

    def has(self, k):
        return self.st >= k or not isinstance(self.dyn, int)


def program(nc, A, O):
    f32, f32r, u32, bf16 = mybir.dt.float32, mybir.dt.float32r, mybir.dt.uint32, mybir.dt.bfloat16
    ALU, ACT, AX = mybir.AluOpType, mybir.ActivationFunctionType, mybir.AxisListType
    ctx = ExitStack()
    with ctx:
        def sb(name, shape, dt=f32):
            return ctx.enter_context(nc.sbuf_tensor(name, shape, dt))

        def sem(name):
            return ctx.enter_context(nc.semaphore(name))

        arena = sb("arena", [P, NKEYS * T])
        raw = sb("raw", [P, RAW, D])
        whi, wlo = sb("whi", [P, 2, D], f32r), sb("wlo", [P, 2, D], f32r)
        mhi, mlo = sb("mhi", [P, C, T], f32r), sb("mlo", [P, C, T], f32r)
        xT = sb("xT", [P, C, T])
        ghi, glo = sb("ghi", [P, 2, T], f32r), sb("glo", [P, 2, T], f32r)
        oneI = sb("oneI", [P, 2, NKEYS, STEP], bf16)
        isJ = sb("isJ", [P, HALF, STEP], bf16)
        gJ = sb("gJ", [P, 2, 3, HALF, STEP], bf16)
        route = sb("route", [P, 4, T], bf16)
        slotI = sb("slotI", [P, T + STEP], bf16)
        iota8 = sb("iota8", [P, NKEYS, STEP], bf16)
        ident, ones, iota = sb("ident", [P, P]), sb("ones", [P, P]), sb("iota", [P, P])
        kept_c = nc.dram_tensor("kept_c", (1, D), f32, kind="Internal").ap()
        modv = sb("modv", [P, LAYERS, MODC])
        bmod = sb("bmod", [P, LAYERS, MODC])
        norms = sb("norms", [P, LAYERS, 2, C])
        modt = sb("modt", [P, MODC])
        modt8 = sb("modt8", [P, 8])
        gainA = sb("gainA", [P, C])
        small = sb("small", [P, 64])

        def carve(at):
            place = [at]

            def take(*shape, dt=f32):
                n = int(np.prod(shape))
                v = arena[:, place[0]:place[0] + n]
                place[0] += n
                assert place[0] <= NKEYS * T
                if dt != f32:
                    v = v.bitcast(dt)
                if len(shape) == 2:
                    v = v.rearrange("p (a b) -> p a b", a=shape[0])
                elif len(shape) == 3:
                    v = v.rearrange("p (a b c) -> p a b c", a=shape[0], b=shape[1])
                elif len(shape) == 4:
                    v = v.rearrange("p (a b c d) -> p a b c d", a=shape[0], b=shape[1], c=shape[2])
                return v
            return take, place

        low, _ = carve(0)
        modw = low(4, 2, D)
        junk, cact = low(D), low(D)
        yT = low(C, T)
        uT, gv, vn = low(GM, T), low(TT, GM, P), low(TT, GM, P)
        vg = low(GM, P)
        high, at_high = carve(NKEYS * T // 2)
        hf, sq = high(C, T), high(C, T)
        gsq = carve(NKEYS * T // 2)[0](TT * GM, P)
        vt, sd = high(T), high(T)
        qk_raw, qk, vbuf = high(2, 2, T), high(2, 2, T), high(2, TT, P)
        sqqk, rstd, qn, rot = high(2, T), high(2, T), high(2, T), high(2, T)
        st_, pr, aT = high(2, 384), high(2, 384), high(2, 384)
        blk64, rotM, ropeC, ropeS = high(P), high(P), high(T), high(T)
        negU, negones, maskKQ, maskQK, gmask = high(P), high(P), high(P), high(P), high(P)
        wsT, bs = high(GM, P), high(GM, P)
        assert at_high[0] <= 30720
        subk = carve(30720)[0](2 * HEADS, P)
        AFTER_NORM = NKEYS * T // 2 + 2 * C * T + 2 * T
        scores = carve(AFTER_NORM)[0](HEADS, TT, 2, P)
        qT = carve(AFTER_NORM + 4096)[0](2 * HEADS, T)
        high, at_high = carve(AFTER_NORM + 4096)
        cur, cur2 = high(TT, 2, P), high(TT, 2, P)
        v16, i16 = high(TT, 2, TOPK), high(TT, 2, TOPK, dt=u32)
        cand, cand2 = high(TT, TOPK, TOPK), high(TT, TOPK, TOPK)
        best, pos = high(TT, TOPK), high(TT, TOPK, dt=u32)
        posA, posB = high(TT, TOPK, dt=u32), high(TT, TOPK, dt=u32)
        eq = high(TT, TOPK, TOPK)
        bestS, keyI, keyJ = high(TT, HEADS, TOPK), high(TT, HEADS, TOPK), high(TT, HEADS, TOPK)
        ssum = high(TT, HEADS)
        rest = high(T)
        assert at_high[0] <= 30720
        ysb = carve(NKEYS * T // 2)[0](TT, D)

        bank = [ctx.enter_context(nc.psum_tensor(f"bank{b}", [P, 512], f32)) for b in range(8)]

        def stream_bank(t):
            return bank[4 + t.slot][:, 0:T]

        const_in, mix_in, subk_in = sem("const_in"), sem("mix_in"), sem("subk_in")
        raw_in = [sem(f"raw_in{s}") for s in range(RAW)]
        mod_in = [sem(f"mod_in{s}") for s in range(4)]
        mod_used = sem("mod_used")
        hi_done, lo_done, tile_done = sem("hi_done"), sem("lo_done"), sem("tile_done")
        act_evac = sem("act_evac")
        ghi_done, glo_done = sem("ghi_done"), sem("glo_done")
        oneI_done, gJ_done, w_done, w_used = sem("oneI_done"), sem("gJ_done"), sem("w_done"), sem("w_used")
        dve_own, act_own, pool_own = sem("dve_own"), sem("act_own"), sem("pool_own")
        dve_body = sem("dve_body")
        exp_c, c_ready, c_kept, c_back = sem("exp_c"), sem("c_ready"), sem("c_kept"), sem("c_back")
        sq_ready, ss_ready, var_ready, sd_ready = sem("sq_ready"), sem("ss_ready"), sem("var_ready"), sem("sd_ready")
        h_ready, mhi_ready, m_ready, x_ready = sem("h_ready"), sem("mhi_ready"), sem("m_ready"), sem("x_ready")
        gvar, gsd, vn_ready, mixed, ya_ready = (sem(n) for n in ("gvar", "gsd", "vn_ready", "mixed", "ya_ready"))
        qsq, qss, qvar, qsd, qn_ready, qrot, qk_ready = (sem(n) for n in (
            "qsq", "qss", "qvar", "qsd", "qn_ready", "qrot", "qk_ready"))
        z_ready, s_sub, s_exp, p_ready, pT_ready, a_ready, yp_ready, y_ready = (sem(n) for n in (
            "z_ready", "s_sub", "s_exp", "p_ready", "pT_ready", "a_ready", "yp_ready", "y_ready"))
        z_ln, sp_ready, cum_ready = sem("z_ln"), sem("sp_ready"), sem("cum_ready")
        sc_ready, sc_used, best_ready, bexp, gates_ready, routeT = (sem(n) for n in (
            "sc_ready", "sc_used", "best_ready", "bexp", "gates_ready", "routeT"))
        y_copied, yT_ready, out_done = sem("y_copied"), sem("yT_ready"), sem("out_done")

        base, acts = [], []
        n = a = 0
        for l in range(LAYERS):
            b, ae = {}, {}
            for name, tiles, by in (("proj", EVEN_T if l == 0 else ODD_T, "a"), ("out", OUT_T, "d"),
                                    ("wq", WQ_T, "a"), ("u", NKEYS, "a"), ("v", NKEYS, "")):
                b[name], ae[name] = n, a
                n += tiles
                a += tiles if by == "a" else 0
            base.append(b)
            acts.append(ae)
        SRC = [{"proj": A["even_in"], "out": A["even_out"]}, {"proj": A["odd_in"], "out": A["odd_out"]}]

        block = ctx.enter_context(nc.Block())

        @block.sync
        def _(sp):
            def load(t, src):
                if t.has(RAW):
                    sp.wait_ge(lo_done, t.count(1 - RAW))
                sp.dma_start(raw[:, t.slot, :], src).then_inc(raw_in[t.slot], 16)

            def load_all(src, first, count, body=RAW):
                with sp.Fori(0, count // body) as i:
                    for s in range(body):
                        load(Tile(first + s, i * body), src[i * body + s])

            for dst, name in ((xT[:, :, :], "xT"), (norms[:, :, :, :], "norms"), (bmod[:, :, :], "bmod"),
                              (ident[:, :], "ident"), (ones[:, :], "ones"), (iota[:, :], "iota")):
                sp.dma_start(dst, A[name]).then_inc(const_in, 16)
            sp.dma_start(cact, A["c"].broadcast_to([P, D])).then_inc(const_in, 16)
            for l in range(LAYERS):
                b = base[l]
                proj, out = SRC[l]["proj"], SRC[l]["out"]
                for s in range(RAW):
                    load(Tile(b["proj"] + s), proj[s])
                if l:
                    sp.wait_ge(x_ready, 16)
                mix = [(maskKQ, "maskKQ"), (negU, "negU"), (negones, "negones")] if l else [
                    (vg.rearrange("p a b -> p (a b)"), "v_gain"), (bs.rearrange("p a b -> p (a b)"), "b_s"),
                    (wsT, "wsT"), (gmask, "gmask"), (blk64, "blk64"), (rotM, "rotM"), (ropeC, "ropeC"),
                    (ropeS, "ropeS"), (maskQK, "maskQK"), (small[:, 0:2], "qk_gain")]
                for dst, name in mix:
                    src = A[name].broadcast_to([P, GM * P]) if name in ("v_gain", "b_s") else A[name]
                    sp.dma_start(dst, src).then_inc(mix_in, 16)
                sp.dma_start(subk, A["subkeys"][l]).then_inc(subk_in, 16)
                for s in range(RAW, EVEN_T if l == 0 else ODD_T):
                    load(Tile(b["proj"] + s), proj[s])
                load_all(out, b["out"], OUT_T)
                load_all(A["w_q"][l], b["wq"], WQ_T)
                load_all(A["u"][l], b["u"], NKEYS)
                load_all(A["v"][l], b["v"], NKEYS)
            sp.wait_ge(x_ready, 32)
            sp.dma_start(O["y"], xT[:, :, :]).then_inc(out_done, 16)
            sp.wait_ge(out_done, 16)

        MIX0, MIX1 = 16 * 10, 16 * 13

        @block.gpsimd
        def _(pool):
            body = Body(pool, pool_own)

            def load_mod(l, q, dyn=0):
                total = l * PAIRS + q
                if total >= 4 or not isinstance(dyn, int):
                    pool.wait_ge(mod_used, 2 * (total - 3 + dyn))
                pool.dma_start(modw[:, total % 4, :, :], A["w_mod"][l, q + dyn]).then_inc(mod_in[total % 4], 16)

            for q in range(4):
                load_mod(0, q)
            pool.wait_ge(c_ready, 1)
            pool.dma_start(kept_c, cact[0:1, :]).then_inc(c_kept, 16)
            with pool.Fori(1, PAIRS // 4) as i:
                for s in range(4):
                    load_mod(0, s, 4 * i)

            for l in range(LAYERS):
                if l == 0:
                    pool.wait_ge(tile_done, base[0]["v"] + HALF)
                    pool.wait_ge(c_kept, 16)
                    pool.dma_start(cact, kept_c.broadcast_to([P, D])).then_inc(c_back, 16)
                    for q in range(4):
                        load_mod(1, q)
                    with pool.Fori(1, PAIRS // 4) as i:
                        for s in range(4):
                            load_mod(1, s, 4 * i)

        @block.scalar
        def _(act):
            own = Count()

            def hi(t):
                act.wait_ge(raw_in[t.slot], t.loaded())
                if t.has(2):
                    act.wait_ge(tile_done, t.count(-1))
                act.activation(whi[:, t.pair, :], raw[:, t.slot, :], ACT.Copy).then_inc(hi_done, 1)

            def evac(t, out, func=ACT.Copy, scale=1.0):
                act.wait_ge(tile_done, t.count(1))
                src = stream_bank(t)
                if len(out.shape) == 3:
                    src = src.rearrange("p (a b) -> p a b", a=TT)
                act.activation(out, src, func, scale=scale).then_inc(act_evac, 1)

            def norm(k):
                if k == 0:
                    act.wait_ge(const_in, 16 * 7)
                else:
                    act.wait_ge(x_ready, 8 * k)
                act.activation(sq, xT[:, :, :], ACT.Square).then_inc(sq_ready, 1)
                act.wait_ge(var_ready, k + 1)
                act.activation(sd, vt, ACT.Sqrt).then_inc(sd_ready, 1)
                for half in range(2):
                    act.wait_ge(h_ready, 2 * k + half + 1)
                    act.activation(mhi[:, 4 * half:4 * half + 4, :], hf[:, 4 * half:4 * half + 4, :],
                                   ACT.Copy).then_inc(mhi_ready, 1)

            act.wait_ge(const_in, 16 * 7)
            act.activation(junk, cact, ACT.Exp, scale=-1.0).then_inc(exp_c, 1)
            for l in range(LAYERS):
                b = base[l]
                norm(2 * l)
                pj = b["proj"]
                outs = []
                if l == 0:
                    outs += [(gv[:, :, g, :], ACT.Gelu_apprx_tanh, 1.0) for g in range(GM)]
                    outs += [(uT[:, g, :], ACT.Gelu_apprx_tanh, 1.0) for g in range(GM)]
                pairs = 4 if l == 0 else 8
                for p in range(pairs):
                    q_to = qk_raw if l == 0 else qk
                    outs += [(q_to[:, p % 2, 0, :], ACT.Copy, 0.125 if l else 1.0), (q_to[:, p % 2, 1, :], ACT.Copy, 1.0),
                             (vbuf[:, p % 2, :, :], ACT.Copy, 1.0)]
                first = len(outs) - 3 * pairs
                if l:
                    act.preload_act_table_set("natural_log_exp_and_others")

                def step(s):
                    if s < len(outs):
                        hi(Tile(pj + s))
                    if 2 <= s < len(outs) + 2:
                        k = s - 2 - first
                        if k >= 6:
                            act.wait_ge(y_ready, 4 * l + k // 3 - 1)
                        evac(Tile(pj + s - 2), *outs[s - 2])

                for s in range(first + 3):
                    step(s)
                    if l == 0 and s == 6:
                        act.wait_ge(gvar, 1)
                        act.activation(small[:, 16:24], small[:, 8:16], ACT.Sqrt).then_inc(gsd, 1)
                for p in range(pairs):
                    s, e = first + 3 * p + 3, 4 * l + p + 1
                    step(s)
                    if l == 0:
                        act.wait_ge(act_evac, acts[0]["proj"] + s - 1)
                        act.activation(sqqk, qk_raw[:, p % 2, :, :], ACT.Square).then_inc(qsq, 1)
                        step(s + 1)
                        act.wait_ge(qvar, p + 1)
                        act.activation(rstd, sqqk, ACT.Sqrt).then_inc(qsd, 1)
                        step(s + 2)
                        act.wait_ge(s_sub, e)
                        act.activation(pr, st_, ACT.Exp, scale=0.125).then_inc(s_exp, 1)
                        for h in range(2):
                            act.wait_ge(pT_ready, 2 * p + h + 1)
                            act.activation(aT[:, h, :], bank[h][:, 0:384], ACT.Copy).then_inc(a_ready, 1)
                    else:
                        step(s + 1)
                        act.wait_ge(z_ready, e)
                        for h in range(2):
                            ins = act.activation(pr[:, h, :], bank[h][:, 0:384], ACT.Abs)
                        ins.then_inc(act_own, 1)
                        act.wait_ge(act_own, own.add())
                        act.activation(pr, pr, ACT.Exp, scale=-1.0).then_inc(act_own, 1)
                        act.wait_ge(act_own, own.add())
                        act.activation(pr, pr, ACT.Ln, bias=1.0).then_inc(z_ln, 1)
                        step(s + 2)
                        for h in range(2):
                            act.wait_ge(cum_ready, 2 * p + h + 1)
                            act.activation(aT[:, h, :], bank[h][:, 0:384], ACT.Exp).then_inc(a_ready, 1)
                    act.wait_ge(yp_ready, e)
                    c = (GM if l == 0 else 0) + p
                    act.activation(yT[:, c, :], bank[2][:, 0:T], ACT.Copy).then_inc(y_ready, 1)
                act.wait_ge(y_ready, 4 * l + pairs)
                if l == 0:
                    act.wait_ge(ya_ready, 1)
                act.activation(mhi[:, :, :], yT, ACT.Copy).then_inc(mhi_ready, 1)
                for s in range(OUT_T):
                    hi(Tile(b["out"] + s))
                norm(2 * l + 1)

                def wq(s, dyn, lag=True):
                    hi(Tile(b["wq"] + s, dyn))
                    if lag:
                        evac(Tile(b["wq"] + s - 2, dyn), qT[:, s - 2 + dyn, :])
                for s in range(4):
                    wq(s, 0, s >= 2)
                with act.Fori(1, WQ_T // 4) as i:
                    for s in range(4):
                        wq(s, 4 * i)
                for s in range(WQ_T - 2, WQ_T):
                    evac(Tile(b["wq"] + s), qT[:, s, :])
                for h in range(HEADS):
                    act.wait_ge(sc_ready, HEADS * l + h + 1)
                    act.activation(scores[:, h, :, :, :].rearrange("p a b c -> p (a b c)"), bank[h % 4][:, :],
                                   ACT.Copy).then_inc(sc_used, 1)

                def u_step(s, dyn, lag=True):
                    hi(Tile(b["u"] + s, dyn))
                    if lag:
                        evac(Tile(b["u"] + s - 2, dyn), arena[:, bass.ds((s - 2) * T + dyn * T, T)],
                             ACT.Gelu_apprx_tanh)
                for s in range(4):
                    u_step(s, 0, s >= 2)
                with act.Fori(1, HALF // 4) as i:
                    for s in range(4):
                        u_step(s, 4 * i)
                act.wait_ge(best_ready, l + 1)
                act.activation(bestS, bestS, ACT.Exp).then_inc(bexp, 1)
                with act.Fori(HALF // 4, NKEYS // 4) as i:
                    for s in range(4):
                        u_step(s, 4 * i)
                for s in range(NKEYS - 2, NKEYS):
                    evac(Tile(b["u"] + s), arena[:, s * T:(s + 1) * T], ACT.Gelu_apprx_tanh)

                for half in range(2):
                    with act.Fori(half * HALF // 4, (half + 1) * HALF // 4) as i:
                        for s in range(4):
                            t = Tile(b["v"] + s, 4 * i)
                            if s == 0:
                                act.wait_ge(w_used, 128 * l + 64 * (half + 1))
                            act.wait_ge(tile_done, t.count(-1))
                            act.activation(ghi[:, t.pair, :], arena[:, bass.ds(s * T + i * (4 * T), T)],
                                           ACT.Copy).then_inc(ghi_done, 1)
                            hi(t)
                act.wait_ge(tile_done, b["v"] + NKEYS)
                for k in range(4):
                    act.activation(ysb[:, k // 2, 512 * (k % 2):512 * (k % 2) + 512], bank[4 + k][:, :],
                                   ACT.Copy).then_inc(y_copied, 1)

        @block.vector
        def _(dve):
            own = Count()

            def seq(ins):
                ins.then_inc(dve_own, 1)
                dve.wait_ge(dve_own, own.add())

            def lo(t):
                dve.wait_ge(hi_done, t.count(1))
                dve.tensor_tensor(wlo[:, t.pair, :], raw[:, t.slot, :], whi[:, t.pair, :].bitcast(f32),
                                  ALU.subtract).then_inc(lo_done, 1)

            def mod_pair(total, col, dyn=0):
                dve.wait_ge(mod_in[total % 4], 16 * (total // 4 + 1) + 4 * dyn)
                for r in range(2):
                    if total or r:
                        dve.wait_ge(mod_used, 2 * (total + dyn) + r)
                    dve.scalar_tensor_tensor(junk, modw[:, total % 4, r, :], 1.0, cact, ALU.mult, ALU.mult,
                                             accum_out=col[:, r:r + 1]).then_inc(mod_used, 1)

            def mod_add(l, a, b_, src):
                seq(dve.tensor_tensor(modv[:, l, a:b_], src[:, a:b_], bmod[:, l, a:b_], ALU.add))

            def norm(l, w):
                k = 2 * l + w
                sh, sc = 3 * C * w, 3 * C * w + C
                seq(dve.scalar_tensor_tensor(gainA[:, :], modv[:, l, sc:sc + C], 1.0, norms[:, l, w, :], ALU.add,
                                             ALU.mult))
                dve.wait_ge(ss_ready, k + 1)
                dve.tensor_scalar(vt, bank[2][:, 0:T], 1.0 / D, EPS, ALU.mult, ALU.add).then_inc(var_ready, 1)
                dve.wait_ge(sd_ready, k + 1)
                seq(dve.reciprocal(vt, sd))
                seq(dve.tensor_tensor(hf, xT[:, :, :], vt.unsqueeze(1).broadcast_to([P, C, T]), ALU.mult))
                for c in range(C):
                    ins = dve.tensor_scalar(hf[:, c, :], hf[:, c, :], gainA[:, c:c + 1],
                                            modv[:, l, sh + c:sh + c + 1], ALU.mult, ALU.add)
                    if c % 4 == 3:
                        ins.then_inc(h_ready, 1)
                for half in range(2):
                    cs = slice(4 * half, 4 * half + 4)
                    dve.wait_ge(mhi_ready, 5 * l + 3 * w + half + 1)
                    dve.tensor_tensor(mlo[:, cs, :], hf[:, cs, :], mhi[:, cs, :].bitcast(f32),
                                      ALU.subtract).then_inc(m_ready, 1)

            dve.wait_ge(exp_c, 1)
            dve.tensor_copy(iota8[:, :, :], iota[:, :].unsqueeze(2).broadcast_to([P, NKEYS, STEP]))
            seq(dve.tensor_scalar(junk, junk, 1.0, None, ALU.add))
            seq(dve.reciprocal(junk, junk))
            dve.tensor_tensor(cact, cact, junk, ALU.mult).then_inc(c_ready, 1)
            dve.wait_ge(c_ready, 1)
            for q in range(8):
                mod_pair(q, modt[:, 2 * q:2 * q + 2])
            dve.wait_ge(mod_used, 16)
            mod_add(0, 0, 2 * C, modt)
            for l in range(LAYERS):
                b = base[l]
                norm(l, 0)
                pj = b["proj"]
                pairs = 4 if l == 0 else 8
                mods = list(range(8, PAIRS)) if l == 0 else []

                def step(s):
                    if s < (EVEN_T if l == 0 else ODD_T):
                        lo(Tile(pj + s))
                    if mods and s >= 2:
                        q = mods.pop(0)
                        mod_pair(q, modt[:, 2 * q:2 * q + 2])

                if l == 0:
                    dve.wait_ge(mix_in, MIX0)
                    seq(dve.tensor_tensor(wsT, wsT, gmask.unsqueeze(1).broadcast_to([P, GM, P]), ALU.mult))
                    for s in range(6):
                        step(s)
                    dve.wait_ge(act_evac, 4)
                    gvf = gv.rearrange("p a b c -> p (a b) c")
                    seq(dve.tensor_tensor(gsq, gvf, gvf, ALU.mult))
                    seq(dve.tensor_reduce(small[:, 8:16], gsq, AX.X, ALU.add))
                    dve.tensor_scalar(small[:, 8:16], small[:, 8:16], 1.0 / P, EPS, ALU.mult,
                                      ALU.add).then_inc(gvar, 1)
                    step(6)
                    step(7)
                    dve.wait_ge(gsd, 1)
                    seq(dve.reciprocal(small[:, 24:32], small[:, 16:24]))
                    seq(dve.tensor_tensor(vn.rearrange("p a b c -> p (a b) c"), gvf,
                                          small[:, 24:32].unsqueeze(2).broadcast_to([P, 8, P]), ALU.mult))
                    dve.tensor_tensor(vn, vn, vg.unsqueeze(1).broadcast_to([P, TT, GM, P]),
                                      ALU.mult).then_inc(vn_ready, 1)
                    step(8)
                    step(9)
                    dve.wait_ge(mixed, 1)
                    dve.wait_ge(act_evac, 8)
                    for g in range(GM):
                        m = bank[g // 2][:, T * (g % 2):T * (g % 2) + T].rearrange("p (a b) -> p a b", a=TT)
                        y = yT[:, g, :].rearrange("p (a b) -> p a b", a=TT)
                        seq(dve.tensor_tensor(y, m, bs[:, g, :].unsqueeze(1).broadcast_to([P, TT, P]), ALU.add))
                        ins = dve.tensor_tensor(yT[:, g, :], yT[:, g, :], uT[:, g, :], ALU.mult)
                    ins.then_inc(ya_ready, 1)
                    step(10)
                else:
                    for s in range(3):
                        step(s)
                first = 8 if l == 0 else 0
                for p in range(pairs):
                    s, e = first + 3 * p + 3, 4 * l + p + 1
                    step(s)
                    if l == 0:
                        dve.wait_ge(qss, p + 1)
                        dve.tensor_scalar(sqqk, bank[3][:, :].rearrange("p (a b) -> p a b", a=2), 1.0 / HEAD, EPS,
                                          ALU.mult, ALU.add).then_inc(qvar, 1)
                        step(s + 1)
                        dve.wait_ge(qsd, p + 1)
                        seq(dve.reciprocal(rstd, rstd))
                        for r in range(2):
                            ins = dve.scalar_tensor_tensor(qn[:, r, :], qk_raw[:, p % 2, r, :], small[:, r:r + 1],
                                                           rstd[:, r, :], ALU.mult, ALU.mult)
                        ins.then_inc(qn_ready, 1)
                        dve.wait_ge(qn_ready, p + 1)
                        seq(dve.tensor_tensor(qk[:, p % 2, :, :], qn, ropeC.unsqueeze(1).broadcast_to([P, 2, T]),
                                              ALU.mult))
                        dve.wait_ge(qrot, p + 1)
                        seq(dve.tensor_tensor(rot, bank[2][:, :].rearrange("p (a b) -> p a b", a=2),
                                              ropeS.unsqueeze(1).broadcast_to([P, 2, T]), ALU.mult))
                        dve.tensor_tensor(qk[:, p % 2, :, :], qk[:, p % 2, :, :], rot, ALU.add).then_inc(qk_ready, 1)
                        step(s + 2)
                        mx, rs = small[:, 32:36], small[:, 36:40]
                        SEG = ((0, P), (P, 384))
                        dve.wait_ge(z_ready, e)
                        for h in range(2):
                            for k, (f, g) in enumerate(SEG):
                                seq(dve.tensor_reduce(mx[:, 2 * h + k:2 * h + k + 1], bank[h][:, f:g], AX.X, ALU.max))
                        for h in range(2):
                            for k, (f, g) in enumerate(SEG):
                                ins = dve.tensor_scalar(st_[:, h, f:g], bank[h][:, f:g],
                                                        mx[:, 2 * h + k:2 * h + k + 1], None, ALU.subtract)
                        ins.then_inc(s_sub, 1)
                        dve.wait_ge(s_exp, e)
                        for k, (f, g) in enumerate(SEG):
                            seq(dve.tensor_reduce(rs[:, 2 * k:2 * k + 2], pr[:, :, f:g], AX.X, ALU.add))
                        seq(dve.reciprocal(rs, rs))
                        for h in range(2):
                            for k, (f, g) in enumerate(SEG):
                                ins = dve.tensor_scalar(pr[:, h, f:g], pr[:, h, f:g], rs[:, 2 * k + h:2 * k + h + 1],
                                                        None, ALU.mult)
                        ins.then_inc(p_ready, 1)
                    else:
                        step(s + 1)
                        dve.wait_ge(z_ln, p + 1)
                        for h in range(2):
                            dve.scalar_tensor_tensor(st_[:, h, :], bank[h][:, 0:384], 0.0, pr[:, h, :], ALU.max,
                                                     ALU.add).then_inc(sp_ready, 1)
                        step(s + 2)
                while mods:
                    step(99)
                if l == 0:
                    dve.wait_ge(mod_used, MODC)
                    mod_add(0, 2 * C, MODC, modt)
                dve.wait_ge(mhi_ready, 5 * l + 3)
                dve.tensor_tensor(mlo[:, :, :], yT, mhi[:, :, :].bitcast(f32), ALU.subtract).then_inc(m_ready, 1)
                for s in range(OUT_T + 2):
                    if s < OUT_T:
                        lo(Tile(b["out"] + s))
                    if s >= 2:
                        t, c = Tile(b["out"] + s - 2), s - 2
                        dve.wait_ge(tile_done, t.count(1))
                        dve.scalar_tensor_tensor(xT[:, c, :], stream_bank(t), modv[:, l, 2 * C + c:2 * C + c + 1],
                                                 xT[:, c, :], ALU.mult, ALU.add).then_inc(x_ready, 1)
                norm(l, 1)
                with dve.Fori(0, WQ_T // 4) as i:
                    for s in range(4):
                        lo(Tile(b["wq"] + s, 4 * i))

                body = Body(dve, dve_body)
                dve.wait_ge(sc_used, HEADS * (l + 1))
                with dve.Fori(0, HEADS) as i:
                    tiles = [Tile(b["u"] + s, 8 * i) for s in range(8)]
                    lo(tiles[0])
                    lo(tiles[1])
                    body.seq(dve.tensor_copy(cur, scores[:, bass.ds(i, 1), :, :, :].squeeze(1)))
                    def top16(lists, between):
                        n = len(lists)
                        for c1, c2, top, idx in lists:
                            body.go(dve.max(top[:, 0:8], c1))
                        for c1, c2, top, idx in lists:
                            body.wait(n - 1)
                            body.go(dve.match_replace(c2, top[:, 0:8], c1, -3e38))
                        between(0)
                        for c1, c2, top, idx in lists:
                            dve.max_index(idx[:, 0:8], top[:, 0:8], c1)
                        for c1, c2, top, idx in lists:
                            body.wait(n - 1)
                            body.go(dve.max(top[:, 8:16], c2))
                        between(1)
                        for c1, c2, top, idx in lists:
                            body.wait(n - 1)
                            body.go(dve.max_index(idx[:, 8:16], top[:, 8:16], c2))

                    def between(first):
                        return lambda k: (lo(tiles[first + 2 * k]), lo(tiles[first + 2 * k + 1]))

                    top16([(cur[:, a, q, :], cur2[:, a, q, :], v16[:, a, q, :], i16[:, a, q, :])
                           for a in range(TT) for q in range(2)], between(2))
                    body.wait()
                    body.seq(dve.tensor_tensor(cand, v16[:, :, 0, :].unsqueeze(3).broadcast_to([P, TT, TOPK, TOPK]),
                                               v16[:, :, 1, :].unsqueeze(2).broadcast_to([P, TT, TOPK, TOPK]),
                                               ALU.add))
                    top16([(cand[:, a, :, :].rearrange("p a b -> p (a b)"),
                            cand2[:, a, :, :].rearrange("p a b -> p (a b)"), best[:, a, :], pos[:, a, :])
                           for a in range(TT)], lambda k: lo(tiles[6 + k]))
                    body.wait()
                    dve.tensor_scalar(posA, pos, 4, None, ALU.logical_shift_right)
                    body.seq(dve.tensor_scalar(posB, pos, TOPK - 1, None, ALU.bitwise_and))
                    for q, (at, key) in enumerate(((posA, keyI), (posB, keyJ))):
                        shape = [P, TT, TOPK, TOPK]
                        row = iota[:, 0:TOPK].unsqueeze(1).unsqueeze(1).broadcast_to(shape)
                        body.seq(dve.tensor_tensor(eq, row, at.unsqueeze(3).broadcast_to(shape), ALU.is_equal))
                        body.seq(dve.tensor_tensor(eq, eq, i16[:, :, q, :].unsqueeze(2).broadcast_to(shape), ALU.mult))
                        body.seq(dve.tensor_reduce(key[:, :, bass.ds(i, 1), :].squeeze(2), eq, AX.X, ALU.add))
                    body.seq(dve.tensor_copy(bestS[:, :, bass.ds(i, 1), :].squeeze(2), best))
                    body.end()
                bshape = [P, TT, HEADS, TOPK]
                seq(dve.tensor_copy(ssum, bestS[:, :, :, 0]))
                dve.tensor_tensor(bestS, bestS, ssum.unsqueeze(3).broadcast_to(bshape),
                                  ALU.subtract).then_inc(best_ready, 1)
                dve.wait_ge(bexp, l + 1)
                seq(dve.tensor_reduce(ssum, bestS, AX.X, ALU.add))
                seq(dve.reciprocal(ssum, ssum))
                dve.tensor_tensor(bestS, bestS, ssum.unsqueeze(3).broadcast_to(bshape),
                                  ALU.mult).then_inc(gates_ready, 1)
                dve.wait_ge(routeT, l + 1)
                seq(dve.tensor_copy(slotI[:, 0:T], bank[2][:, 0:T]))
                dve.tensor_copy(slotI[:, T:T + STEP], slotI[:, 0:STEP])
                dve.tensor_copy(route[:, 0, :], bank[2][:, T:2 * T])
                seq(dve.tensor_copy(route[:, 1, :], bank[3][:, 0:T]))
                seq(dve.tensor_tensor(rest, bank[3][:, 0:T], route[:, 1, :], ALU.subtract))
                seq(dve.tensor_copy(route[:, 2, :], rest))
                seq(dve.tensor_tensor(rest, rest, route[:, 2, :], ALU.subtract))
                seq(dve.tensor_copy(route[:, 3, :], rest))

                def first_keys(k, dyn=0):
                    if k >= 2 or not isinstance(dyn, int):
                        dve.wait_ge(w_done, 128 * l + 2 * (k - 1) + 2 * dyn)
                    t0 = STEP * (k if k <= STEPS else k - STEPS) + STEP * dyn
                    shape = [P, NKEYS, STEP]
                    dve.tensor_tensor(oneI[:, k % 2, :, :], iota8[:, :, :],
                                      slotI[:, bass.ds(t0, STEP)].unsqueeze(1).broadcast_to(shape),
                                      ALU.is_equal).then_inc(oneI_done, 1)

                def second_keys(k, dyn, half):
                    n = STEPS * (2 * l + half) + k
                    if n or not isinstance(dyn, int):
                        dve.wait_ge(gJ_done, 3 * n + 3 * dyn)
                    shape = [P, HALF, STEP]
                    row = route[:, 0, bass.ds(STEP * k + STEP * dyn, STEP)].unsqueeze(1).broadcast_to(shape)
                    body.go(dve.tensor_tensor(isJ[:, :, :], iota8[:, HALF * half:HALF * (half + 1), :], row,
                                              ALU.is_equal))

                def gated(k, dyn, half):
                    n = STEPS * (2 * l + half) + k
                    body.wait()
                    if n >= 2 or not isinstance(dyn, int):
                        dve.wait_ge(w_done, 2 * (n - 1) + 2 * dyn)
                    for part in range(3):
                        g = route[:, 1 + part, bass.ds(STEP * k + STEP * dyn, STEP)]
                        dve.tensor_tensor(gJ[:, k % 2, part, :, :], isJ[:, :, :],
                                          g.unsqueeze(1).broadcast_to([P, HALF, STEP]), ALU.mult).then_inc(gJ_done, 1)

                def weigh(g, dyn, half):
                    total = l * 128 + 64 * half + g
                    dve.wait_ge(w_done, total + 1 + dyn)
                    t0 = g * GROUP + GROUP * dyn
                    part = arena[:, HALF * T * half:HALF * T * (half + 1)].rearrange("p (j t) -> p t j", t=T)
                    part = part[:, bass.ds(t0, GROUP), :]
                    w = bank[total % 2][:, 0:GROUP * HALF].rearrange("p (t j) -> p t j", t=GROUP)
                    dve.tensor_tensor(part, w, part, ALU.mult).then_inc(w_used, 1)

                def body_b(i, first):
                    for s in range(4):
                        if s % 2 == 0:
                            second_keys(s // 2, 2 * i, 0)
                        else:
                            first_keys((s + 1) // 2, 2 * i)
                        lo(Tile(b["u"] + HALF + s, 4 * i))
                        if s % 2 == 0:
                            gated(s // 2, 2 * i, 0)
                        if first and s == 1:
                            dve.wait_ge(act_evac, acts[l]["u"] + HALF)
                        if not (first and s == 0):
                            weigh(s - 1, 4 * i, 0)
                    body.end()
                first_keys(0)
                body_b(0, True)
                with dve.Fori(1, 16) as i:
                    body_b(i, False)

                def g_lo(t, j):
                    dve.wait_ge(ghi_done, j + 1)
                    dve.tensor_tensor(glo[:, t.pair, :], arena[:, bass.ds((j - 128 * l) * T, T)],
                                      ghi[:, t.pair, :].bitcast(f32), ALU.subtract).then_inc(glo_done, 1)

                def body_c(i, first):
                    for s in range(4):
                        t = Tile(b["v"] + s, 4 * i)
                        if first and s == 0:
                            weigh(63, 0, 0)
                        if s % 2 == 0:
                            second_keys(s // 2, 2 * i, 1)
                        else:
                            first_keys(STEPS + (s + 1) // 2, 2 * i)
                        g_lo(t, 128 * l + s + 4 * i)
                        lo(t)
                        if s % 2 == 0:
                            gated(s // 2, 2 * i, 1)
                        if first and s == 1:
                            dve.wait_ge(act_evac, acts[l]["u"] + NKEYS)
                        if not (first and s == 0):
                            weigh(s - 1, 4 * i, 1)
                    body.end()
                body_c(0, True)
                with dve.Fori(1, 16) as i:
                    body_c(i, False)
                weigh(63, 0, 1)

                def body_d(dyn):
                    for s in range(8):
                        t = Tile(b["v"] + HALF + s, dyn)
                        g_lo(t, 128 * l + HALF + s + dyn)
                        lo(t)

                if l == 0:
                    dve.wait_ge(c_back, 16)
                    with dve.Fori(0, PAIRS // 4) as i:
                        body_d(8 * i)
                        for q in range(4):
                            mod_pair(PAIRS + q, modt8[:, 2 * q:2 * q + 2], 4 * i)
                        dve.wait_ge(mod_used, MODC + 8 + 8 * i)
                        body.seq(dve.tensor_copy(modt[:, bass.ds(8 * i, 8)], modt8[:, :]))
                        body.end()
                    mod_add(1, 0, MODC, modt)
                    with dve.Fori(PAIRS // 4, HALF // 8) as i:
                        body_d(8 * i)
                else:
                    with dve.Fori(0, HALF // 8) as i:
                        body_d(8 * i)
                for c in range(C):
                    if c % 2 == 0:
                        dve.wait_ge(yT_ready, 4 * l + c // 2 + 1)
                    dve.scalar_tensor_tensor(xT[:, c, :], bank[c // 2][:, T * (c % 2):T * (c % 2) + T],
                                             modv[:, l, 5 * C + c:5 * C + c + 1], xT[:, c, :], ALU.mult,
                                             ALU.add).then_inc(x_ready, 1)

        @block.tensor
        def _(pe):

            def weights(t, swap=False):
                out = stream_bank(t)
                pe.wait_ge(hi_done, t.count(1))
                if swap:
                    for a in range(TT):
                        ms, o = slice(a * P, (a + 1) * P), out[:, a * P:(a + 1) * P]
                        if a == 0:
                            pe.wait_ge(lo_done, t.count(1))
                        for c in range(C):
                            w = slice(c * P, (c + 1) * P)
                            pe.matmul(o, mhi[:, c, ms], whi[:, t.pair, w], start=c == 0, stop=False)
                            pe.matmul(o, mhi[:, c, ms], wlo[:, t.pair, w], start=False, stop=False)
                            ins = pe.matmul(o, mlo[:, c, ms], whi[:, t.pair, w], start=False, stop=c == C - 1)
                else:
                    for c in range(C):
                        w = whi[:, t.pair, c * P:(c + 1) * P]
                        pe.matmul(out, w, mhi[:, c, :], start=c == 0, stop=False)
                        pe.matmul(out, w, mlo[:, c, :], start=False, stop=False)
                    pe.wait_ge(lo_done, t.count(1))
                    for c in range(C):
                        ins = pe.matmul(out, wlo[:, t.pair, c * P:(c + 1) * P], mhi[:, c, :], start=False,
                                        stop=c == C - 1)
                ins.then_inc(tile_done, 1)

            def norm(k):
                pe.wait_ge(sq_ready, k + 1)
                for c in range(C):
                    ins = pe.matmul(bank[2][:, 0:T], ones[:, :], sq[:, c, :], start=c == 0, stop=c == C - 1)
                ins.then_inc(ss_ready, 1)

            pe.wait_ge(const_in, 16 * 7)
            for l in range(LAYERS):
                b = base[l]
                norm(2 * l)
                pe.wait_ge(m_ready, 5 * l + 2)
                pj, ae = b["proj"], acts[l]["proj"]
                if l:
                    pe.wait_ge(y_copied, 4)
                tiles = EVEN_T if l == 0 else ODD_T
                first = 8 if l == 0 else 0
                pairs = 4 if l == 0 else 8

                def step(s):
                    if s >= tiles:
                        return
                    if s >= 4:
                        pe.wait_ge(act_evac, ae + s - 3)
                    weights(Tile(pj + s), swap=(l == 0 and s < GM) or (s >= first and (s - first) % 3 == 2))

                for s in range(first + 3):
                    step(s)
                    if l == 0 and s == 9:
                        pe.wait_ge(vn_ready, 1)
                        for g in range(GM):
                            for a in range(TT):
                                at = T * (g % 2) + a * P
                                ins = pe.matmul(bank[g // 2][:, at:at + P], vn[:, a, g, :], wsT[:, g, :],
                                                start=True, stop=True)
                        ins.then_inc(mixed, 1)
                pe.wait_ge(mix_in, MIX1 if l else MIX0)
                for p in range(pairs):
                    s, e = first + 3 * p + 3, 4 * l + p + 1
                    q, k, v = qk[:, p % 2, 0, :], qk[:, p % 2, 1, :], vbuf[:, p % 2, :, :]
                    heads = [slice(HEAD * h, HEAD * (h + 1)) for h in range(2)]
                    step(s)
                    if l == 0:
                        pe.wait_ge(qsq, p + 1)
                        if p:
                            pe.wait_ge(qvar, p)
                        for r in range(2):
                            ins = pe.matmul(bank[3][:, r * T:(r + 1) * T], blk64, sqqk[:, r, :],
                                            start=True, stop=True)
                        ins.then_inc(qss, 1)
                        step(s + 1)
                        pe.wait_ge(qn_ready, p + 1)
                        if p:
                            pe.wait_ge(y_ready, p)
                        for r in range(2):
                            ins = pe.matmul(bank[2][:, r * T:(r + 1) * T], rotM, qn[:, r, :], start=True, stop=True)
                        ins.then_inc(qrot, 1)
                        pe.wait_ge(qk_ready, p + 1)
                        if p == 0:
                            pe.wait_ge(ya_ready, 1)
                        else:
                            pe.wait_ge(a_ready, 2 * p)
                        for h, hd in enumerate(heads):
                            z = bank[h]
                            pe.matmul(z[:, 0:P], q[hd, 0:P], k[hd, 0:P], start=True, stop=False,
                                      skip_group_check=True)
                            pe.matmul(z[:, 0:P], ident[:, :], maskQK, start=False, stop=False,
                                      skip_group_check=True)
                            pe.matmul(z[:, P:384], q[hd, P:T], k[hd, :], start=False, stop=False,
                                      skip_group_check=True)
                            ins = pe.matmul(z[:, T:384], ident[:, :], maskQK, start=False, stop=True,
                                            skip_group_check=True)
                        ins.then_inc(z_ready, 1)
                        step(s + 2)
                        pe.wait_ge(p_ready, p + 1)
                        for h in range(2):
                            for r in range(3):
                                ins = pe.transpose(bank[h][:, r * P:(r + 1) * P], pr[:, h, r * P:(r + 1) * P],
                                                   ident[:, :])
                            ins.then_inc(pT_ready, 1)
                    else:
                        pe.wait_ge(act_evac, ae + s - 1)
                        pe.wait_ge(a_ready, 2 * (e - 1))
                        for h, hd in enumerate(heads):
                            z = bank[h]
                            pe.matmul(z[:, 0:T], k[hd, 0:P], q[hd, :], start=True, stop=False,
                                      skip_group_check=True)
                            pe.matmul(z[:, 0:P], ident[:, :], maskKQ, start=False, stop=False,
                                      skip_group_check=True)
                            pe.matmul(z[:, T:384], k[hd, P:T], q[hd, P:T], start=False, stop=False,
                                      skip_group_check=True)
                            ins = pe.matmul(z[:, T:384], ident[:, :], maskKQ, start=False, stop=True,
                                            skip_group_check=True)
                        ins.then_inc(z_ready, 1)
                        step(s + 1)
                        for h in range(2):
                            z, sp_ = bank[h], st_[:, h, :]
                            pe.wait_ge(sp_ready, 2 * p + h + 1)
                            pe.matmul(z[:, 0:T], negU, sp_[:, 0:T], start=False, stop=False, skip_group_check=True)
                            pe.matmul(z[:, P:T], negones, sp_[:, T:384], start=False, stop=False,
                                      skip_group_check=True)
                            pe.matmul(z[:, T:384], negU, sp_[:, T:384], start=False, stop=True,
                                      skip_group_check=True).then_inc(cum_ready, 1)
                        step(s + 2)
                    pe.wait_ge(y_ready, e - 1) if e > 1 else None
                    for h, hd in enumerate(heads):
                        pe.wait_ge(a_ready, 2 * (e - 1) + h + 1)
                        yo = bank[2]
                        pe.matmul(yo[hd, 0:T], v[:, 0, hd], aT[:, h, 0:T], start=True, stop=False,
                                  skip_group_check=True)
                        ins = pe.matmul(yo[hd, P:T], v[:, 1, hd], aT[:, h, T:384], start=False, stop=True,
                                        skip_group_check=True)
                    ins.then_inc(yp_ready, 1)

                pe.wait_ge(m_ready, 5 * l + 3)
                for s in range(OUT_T):
                    if s >= 4:
                        pe.wait_ge(x_ready, 16 * l + s - 3)
                    weights(Tile(b["out"] + s))
                norm(2 * l + 1)
                pe.wait_ge(m_ready, 5 * l + 5)

                def ring(name, s, dyn):
                    pe.wait_ge(act_evac, acts[l][name] + s - 3 + dyn)
                    weights(Tile(b[name] + s, dyn))

                with pe.Fori(0, WQ_T // 4) as i:
                    for s in range(4):
                        ring("wq", s, 4 * i)
                pe.wait_ge(act_evac, acts[l]["u"])
                pe.wait_ge(subk_in, 16 * (l + 1))
                for h in range(HEADS):
                    if h >= 4:
                        pe.wait_ge(sc_used, HEADS * l + h - 3)
                    for a in range(TT):
                        for q in range(2):
                            r = (2 * a + q) * P
                            ins = pe.matmul(bank[h % 4][:, r:r + P], qT[:, 2 * h + q, a * P:(a + 1) * P],
                                            subk[:, 2 * h + q, :], start=True, stop=True)
                    ins.then_inc(sc_ready, 1)
                with pe.Fori(0, HALF // 4) as i:
                    for s in range(4):
                        ring("u", s, 4 * i)
                pe.wait_ge(best_ready, l + 1)
                for a in range(TT):
                    for src, at in ((keyI, 0), (keyJ, T)):
                        pe.transpose(bank[2][:, at + a * P:at + (a + 1) * P],
                                     src[:, a, :, :].rearrange("p a b -> p (a b)"), ident[:, :])
                pe.wait_ge(gates_ready, l + 1)
                for a in range(TT):
                    ins = pe.transpose(bank[3][:, a * P:(a + 1) * P], bestS[:, a, :, :].rearrange("p a b -> p (a b)"),
                                       ident[:, :])
                ins.then_inc(routeT, 1)

                def onehot_product(g, dyn, half, half_dyn=0):
                    total = l * 128 + 64 * half + g
                    if g % 2 == 0:
                        k = STEPS * half + g // 2
                        pe.wait_ge(oneI_done, (2 * STEPS + 1) * l + k + 1 + half_dyn)
                        pe.wait_ge(gJ_done, 3 * (2 * STEPS * l + k + 1) + 3 * half_dyn)
                    if total >= 2 or not isinstance(dyn, int):
                        pe.wait_ge(w_used, total - 1 + dyn)
                    two = (g // 2) % 2
                    for k in range(GROUP):
                        out, at = bank[total % 2][:, HALF * k:HALF * (k + 1)], GROUP * (g % 2) + k
                        for part in range(3):
                            ins = pe.matmul(out, oneI[:, two, :, at], gJ[:, two, part, :, at],
                                            start=part == 0, stop=part == 2)
                    ins.then_inc(w_done, 1)

                def body_b(i):
                    for s in range(4):
                        ring("u", HALF + s, 4 * i)
                        onehot_product(s, 4 * i, 0, 2 * i)
                body_b(0)
                with pe.Fori(1, 16) as i:
                    body_b(i)

                def v_tile(s, dyn, start=False, stop=False):
                    t = Tile(b["v"] + s, dyn)
                    vs = [slice(512 * h, 512 * h + 512) for h in range(2)]
                    ts_ = [slice(a * P, (a + 1) * P) for a in range(TT)]
                    pe.wait_ge(hi_done, t.count(1))
                    pe.wait_ge(ghi_done, 128 * l + s + 1 + dyn)
                    for a in range(TT):
                        for h in range(2):
                            pe.matmul(bank[4 + 2 * a + h][:, :], ghi[:, t.pair, ts_[a]], whi[:, t.pair, vs[h]],
                                      start=start, stop=False, skip_group_check=True)
                    pe.wait_ge(glo_done, 128 * l + s + 1 + dyn)
                    for a in range(TT):
                        for h in range(2):
                            pe.matmul(bank[4 + 2 * a + h][:, :], glo[:, t.pair, ts_[a]], whi[:, t.pair, vs[h]],
                                      start=False, stop=False, skip_group_check=True)
                    pe.wait_ge(lo_done, t.count(1))
                    for a in range(TT):
                        for h in range(2):
                            ins = pe.matmul(bank[4 + 2 * a + h][:, :], ghi[:, t.pair, ts_[a]],
                                            wlo[:, t.pair, vs[h]], start=False, stop=stop, skip_group_check=True)
                    return ins.then_inc(tile_done, 1)

                def body_c(i, start):
                    for s in range(4):
                        v_tile(s, 4 * i, start and s == 0)
                        onehot_product(s, 4 * i, 1, 2 * i)
                pe.wait_ge(act_evac, acts[l]["u"] + NKEYS)
                body_c(0, True)
                with pe.Fori(1, 16) as i:
                    body_c(i, False)
                with pe.Fori(16, 31) as i:
                    for s in range(4):
                        v_tile(s, 4 * i)
                for s in range(4):
                    ins = v_tile(NKEYS - 4 + s, 0, False, s == 3)
                for c in range(C):
                    for a in range(TT):
                        if c == 0:
                            pe.wait_ge(y_copied, 4 * l + 2 * a + 1)
                            pe.wait_ge(w_used, 128 * (l + 1))
                        if c == 4:
                            pe.wait_ge(y_copied, 4 * l + 2 * a + 2)
                        at = T * (c % 2) + a * P
                        ins = pe.transpose(bank[c // 2][:, at:at + P], ysb[:, a, c * P:(c + 1) * P], ident[:, :])
                    if c % 2:
                        ins.then_inc(yT_ready, 1)


def constants():
    f = np.float32
    r = np.arange(P)
    q = r % HEAD
    ident = np.eye(P, dtype=f)
    inv = (500000.0 ** (-np.arange(ROPE_HALF, dtype=f) / ROPE_HALF)).astype(f)
    ang = np.arange(T, dtype=f)[None, :] * inv[q % ROPE_HALF][:, None]
    roped = (q < 2 * ROPE_HALF)[:, None]
    rot = np.zeros((P, P), f)
    for m in r:
        if q[m] < ROPE_HALF:
            rot[m + ROPE_HALF, m] = -1
        elif q[m] < 2 * ROPE_HALF:
            rot[m - ROPE_HALF, m] = 1
    return {
        "ident": ident, "ones": np.ones((P, P), f), "iota": np.tile(r.astype(f), (P, 1)),
        "blk64": (r[:, None] // HEAD == r[None, :] // HEAD).astype(f), "rotM": rot,
        "ropeC": np.where(roped, np.cos(ang), 1).astype(f), "ropeS": np.where(roped, np.sin(ang), 0).astype(f),
        "negU": -(r[:, None] >= r[None, :]).astype(f), "negones": -np.ones((P, P), f),
        "maskKQ": np.where(r[:, None] >= r[None, :], NEG, 0).astype(f),
        "maskQK": np.where(r[None, :] > r[:, None], NEG, 0).astype(f),
        "gmask": (r[:, None] <= r[None, :]).astype(f),
    }


def kernel(**inputs):
    import concourse.bacc as bacc
    from concourse.bass_utils import run_bass_kernel_spmd

    x = {k: np.asarray(v) for k, v in inputs.items()}
    pack = np.ascontiguousarray

    def tiles(w):
        return pack(w.reshape(C, P, -1, P).transpose(2, 1, 0, 3)).reshape(-1, P, D)

    def by_pair(w, starts, width):
        return [w[:, s + P * p:s + P * (p + 1)] for p in range(width // P) for s in starts]

    we, wo = x["even_w_in"][0], x["odd_w_in"][0]
    gw = GM * P
    even = np.concatenate([we[:, gw:2 * gw], we[:, 0:gw]] + by_pair(we, [2 * gw, 3 * gw, 4 * gw], gw), axis=1)
    odd = np.concatenate(by_pair(wo, [0, D, 2 * D], D), axis=1)
    gains = np.stack([np.concatenate([x[n][0]] * 2) for n in ("moba_q_gain", "moba_k_gain")], axis=1)
    data = {
        "xT": pack(x["x"][0].T.reshape(C, P, T).transpose(1, 0, 2)), "c": x["c"],
        "w_mod": pack(x["w_mod"].transpose(0, 2, 1).reshape(LAYERS, PAIRS, 2, P, D).transpose(0, 1, 3, 2, 4)),
        "bmod": pack(x["b_mod"].reshape(LAYERS, MODC, P).transpose(2, 0, 1)),
        "norms": pack(np.stack([x["norm_mix"], x["norm_ffn"]], 1).reshape(LAYERS, 2, C, P).transpose(3, 0, 1, 2)),
        "even_in": tiles(even), "even_out": tiles(x["even_w_out"][0]),
        "odd_in": tiles(odd), "odd_out": tiles(x["odd_w_out"][0]),
        "w_q": np.stack([tiles(w) for w in x["peer_w_q"]]),
        "subkeys": pack(x["peer_subkeys"].transpose(0, 4, 1, 2, 3)).reshape(LAYERS, P, 2 * HEADS, P),
        "u": np.stack([pack(u.reshape(P, P, C, P).transpose(1, 3, 2, 0)).reshape(NKEYS, P, D)
                       for u in x["peer_u"]]),
        "v": np.stack([pack(v.reshape(P, P, D).transpose(1, 0, 2)) for v in x["peer_v"]]),
        "v_gain": x["gmlp_v_gain"].reshape(1, gw), "b_s": x["gmlp_b_s"].reshape(1, gw),
        "wsT": pack(x["gmlp_w_s"][0].transpose(2, 0, 1)), "qk_gain": pack(gains),
    }
    data.update(constants())
    nc = bacc.Bacc("TRN2", target_bir_lowering=False, num_devices=1)
    A = {n: nc.dram_tensor(f"in_{n}", a.shape, mybir.dt.float32, kind="ExternalInput").ap() for n, a in data.items()}
    O = {"y": nc.dram_tensor("out_y", (P, C, T), mybir.dt.float32, kind="ExternalOutput").ap()}
    program(nc, A, O)
    r = run_bass_kernel_spmd(nc, [{f"in_{n}": a for n, a in data.items()}], core_ids=[0])
    y = r.results[0]["out_y"]
    return pack(y.transpose(2, 1, 0)).reshape(1, T, D)
```

```python
from contextlib import ExitStack

import numpy as np

import concourse.bass as bass
from concourse import mybir

D, T, P = 1024, 256, 128
C = D // P
TT = T // P
HEADS, TOPK, NKEYS = 8, 16, 128
MODC = 6 * C
HALF = NKEYS // 2
GROUP, STEP = 4, 8
STEPS = T // STEP
EVEN_T, ODD_T, OUT_T, WQ_T = 20, 24, 8, 16
GM = 4
LAYERS = 2
ROPE_HALF, HEAD = 8, 64
EPS = 1e-6
NEG = -1e30
RAW = 4
MOD_FIRST, MOD_MIX, MOD_WQ, MOD_D, MOD_ALL = 8, 12, 4, 12, LAYERS * MODC // 2
BEFORE_D = MOD_FIRST + MOD_MIX + MOD_WQ
BEFORE_MIX1 = BEFORE_D + MOD_D
AHEAD = 6


def projection_order(l):
    order = []
    if l == 0:
        order += [(half, g) for g in range(GM // 2) for half in ("ga", "gb")] + [("u", g) for g in range(GM)]
    for d in range(2 if l == 0 else 4):
        order += [("va", d), ("vb", d), ("q", 2 * d), ("k", 2 * d), ("q", 2 * d + 1), ("k", 2 * d + 1)]
    return order


def above(n, dyn, least):
    return not isinstance(dyn, int) or n + dyn >= least


class Count:

    def __init__(self):
        self.n = 0

    def add(self, k=1):
        self.n += k
        return self.n


class Body:

    def __init__(self, eng, sem):
        self.eng, self.sem, self.n = eng, sem, 0

    def seq(self, ins):
        self.n += 1
        ins.then_inc(self.sem, 1)
        self.wait()

    def go(self, ins):
        self.n += 1
        ins.then_inc(self.sem, 1)

    def wait(self, back=0):
        self.eng.wait_ge(self.sem, self.n - back)

    def end(self):
        self.eng.sem_clear(self.sem)
        self.n = 0


class Tile:

    def __init__(self, first, dyn=0):
        self.st, self.dyn = first, dyn
        self.slot, self.pair = first % RAW, first % 2

    def count(self, k=0):
        return self.st + k + self.dyn

    def loaded(self):
        return 16 * (self.st // RAW + 1) + (16 // RAW) * self.dyn

    def has(self, k):
        return self.st >= k or not isinstance(self.dyn, int)


def program(nc, A, O):
    f32, f32r, u32, bf16 = mybir.dt.float32, mybir.dt.float32r, mybir.dt.uint32, mybir.dt.bfloat16
    ALU, ACT, AX = mybir.AluOpType, mybir.ActivationFunctionType, mybir.AxisListType
    ctx = ExitStack()
    with ctx:
        def sb(name, shape, dt=f32):
            return ctx.enter_context(nc.sbuf_tensor(name, shape, dt))

        def sem(name):
            return ctx.enter_context(nc.semaphore(name))

        arena = sb("arena", [P, NKEYS * T])
        raw = sb("raw", [P, RAW, D])
        whi, wlo = sb("whi", [P, 2, D], f32r), sb("wlo", [P, 2, D], f32r)
        mhi, mlo = sb("mhi", [P, C, T], f32r), sb("mlo", [P, C, T], f32r)
        xT = sb("xT", [P, C, T])
        ghi, glo = sb("ghi", [P, 2, T], f32r), sb("glo", [P, 2, T], f32r)
        oneI = sb("oneI", [P, 2, NKEYS, STEP], bf16)
        isJ = sb("isJ", [P, HALF, STEP], bf16)
        gJ = sb("gJ", [P, 2, 3, HALF, STEP], bf16)
        route = sb("route", [P, 4, T], bf16)
        slotI = sb("slotI", [P, T + STEP], bf16)
        iota8 = sb("iota8", [P, NKEYS, STEP], bf16)
        ident, ones, iota = sb("ident", [P, P]), sb("ones", [P, P]), sb("iota", [P, P])
        kept_c = nc.dram_tensor("kept_c", (1, D), f32, kind="Internal").ap()
        modv = sb("modv", [P, LAYERS, MODC])
        bmod = sb("bmod", [P, LAYERS, MODC])
        norms = sb("norms", [P, LAYERS, 2, C])
        modt = sb("modt", [P, LAYERS * MODC])
        eps = sb("eps", [P, 1])
        modt8 = sb("modt8", [P, 8])
        gainA = sb("gainA", [P, C])
        small = sb("small", [P, 64])

        def carve(at):
            place = [at]

            def take(*shape, dt=f32):
                n = int(np.prod(shape))
                v = arena[:, place[0]:place[0] + n]
                place[0] += n
                assert place[0] <= NKEYS * T
                if dt != f32:
                    v = v.bitcast(dt)
                if len(shape) == 2:
                    v = v.rearrange("p (a b) -> p a b", a=shape[0])
                elif len(shape) == 3:
                    v = v.rearrange("p (a b c) -> p a b c", a=shape[0], b=shape[1])
                elif len(shape) == 4:
                    v = v.rearrange("p (a b c d) -> p a b c d", a=shape[0], b=shape[1], c=shape[2])
                return v
            return take, place

        low, _ = carve(0)
        modw = low(4, 2, D)
        junk, cact = low(D), low(D)
        yT = low(C, T)
        uT, gv, vn = low(GM, T), low(TT, GM, P), low(TT, GM, P)
        vg = low(GM, P)
        high, at_high = carve(NKEYS * T // 2)
        hf, sq = high(C, T), high(C, T)
        gsq = carve(NKEYS * T // 2)[0](TT * GM, P)
        rs = high(T)
        qk_raw, qk, vbuf = high(2, 2, T), high(2, 2, T), high(2, 2, TT, P)
        sqqk, rstd, qn, rot = high(2, T), high(2, T), high(2, T), high(2, T)
        st_, pr, aT = high(2, 384), high(2, 384), high(2, 384)
        blk64, rotM, ropeC, ropeS = high(P), high(P), high(T), high(T)
        negU, negones, maskKQ, maskQK, gmask = high(P), high(P), high(P), high(P), high(P)
        wsT, bs = high(GM, P), high(GM, P)
        assert at_high[0] <= 30720
        subk = carve(30720)[0](2 * HEADS, P)
        AFTER_NORM = NKEYS * T // 2 + 2 * C * T + 2 * T
        scores = carve(AFTER_NORM)[0](HEADS, TT, 2, P)
        qT = carve(AFTER_NORM + 4096)[0](2 * HEADS, T)
        high, at_high = carve(AFTER_NORM + 4096)
        cur, cur2 = high(TT, 2, P), high(TT, 2, P)
        v16, i16 = high(TT, 2, TOPK), high(TT, 2, TOPK, dt=u32)
        cand, cand2 = high(TT, TOPK, TOPK), high(TT, TOPK, TOPK)
        best, pos = high(TT, TOPK), high(TT, TOPK, dt=u32)
        posA, posB = high(TT, TOPK, dt=u32), high(TT, TOPK, dt=u32)
        keys, places = high(TT, 2, TOPK), high(TT, 2, TOPK)
        eq, picked = high(TT, TOPK, TOPK), high(TT, TOPK)
        bestS, keyI, keyJ = high(TT, HEADS, TOPK), high(TT, HEADS, TOPK), high(TT, HEADS, TOPK)
        ssum = high(TT, HEADS)
        rest = high(T)
        assert at_high[0] <= 30720
        ysb = carve(NKEYS * T // 2)[0](TT, D)

        bank = [ctx.enter_context(nc.psum_tensor(f"bank{b}", [P, 512], f32)) for b in range(8)]

        def stream_bank(t):
            return bank[4 + t.slot][:, 0:T]

        def norm_bank(k):
            return bank[0 if k == 2 else 2]

        const_in, mix_in, subk_in = sem("const_in"), sem("mix_in"), sem("subk_in")
        raw_in = [sem(f"raw_in{s}") for s in range(RAW)]
        mod_in = [sem(f"mod_in{s}") for s in range(4)]
        mod_first_in = [sem(f"mod_first_in{s}") for s in range(4)]
        mod_used, c_in, eps_ready = sem("mod_used"), sem("c_in"), sem("eps_ready")
        hi_done, lo_done, tile_done = sem("hi_done"), sem("lo_done"), sem("tile_done")
        act_evac = sem("act_evac")
        ghi_done, glo_done = sem("ghi_done"), sem("glo_done")
        oneI_done, gJ_done, w_done, w_used = sem("oneI_done"), sem("gJ_done"), sem("w_done"), sem("w_used")
        dve_own, act_own, pool_own = sem("dve_own"), sem("act_own"), sem("pool_own")
        dve_body = sem("dve_body")
        exp_c, c_ready, c_kept, c_back = sem("exp_c"), sem("c_ready"), sem("c_kept"), sem("c_back")
        sq_ready, ss_ready, rs_ready = sem("sq_ready"), sem("ss_ready"), sem("rs_ready")
        h_ready, mhi_ready, m_ready, x_ready = sem("h_ready"), sem("mhi_ready"), sem("m_ready"), sem("x_ready")
        gvar, gsd, vn_ready, mixed, ya_ready = (sem(n) for n in ("gvar", "gsd", "vn_ready", "mixed", "ya_ready"))
        qsq, qss, qsd, qn_ready, qrot, qk_ready = (sem(n) for n in (
            "qsq", "qss", "qsd", "qn_ready", "qrot", "qk_ready"))
        z_ready, s_sub, s_exp, p_ready, pT_ready, a_ready, yp_ready, y_ready = (sem(n) for n in (
            "z_ready", "s_sub", "s_exp", "p_ready", "pT_ready", "a_ready", "yp_ready", "y_ready"))
        z_ln, sp_ready, cum_ready = sem("z_ln"), sem("sp_ready"), sem("cum_ready")
        cur_ready, cur_used, picks_ready, keys_done = (sem(n) for n in (
            "cur_ready", "cur_used", "picks_ready", "keys_done"))
        sc_ready, sc_used, best_ready, bexp, gates_ready, routeT = (sem(n) for n in (
            "sc_ready", "sc_used", "best_ready", "bexp", "gates_ready", "routeT"))
        y_copied, yT_ready, out_done = sem("y_copied"), sem("yT_ready"), sem("out_done")

        base, acts = [], []
        n = a = 0
        for l in range(LAYERS):
            b, ae = {}, {}
            for name, tiles, by in (("proj", EVEN_T if l == 0 else ODD_T, "a"), ("out", OUT_T, "d"),
                                    ("wq", WQ_T, "a"), ("u", NKEYS, "a"), ("v", NKEYS, "")):
                b[name], ae[name] = n, a
                n += tiles
                a += tiles if by == "a" else 0
            base.append(b)
            acts.append(ae)
        def z_bank(p, h):
            return bank[2 * (p % 2) + h]

        def k_taken(l, p):
            return acts[l]["proj"] + projection_order(l).index(("k", p)) + 1

        SRC = [{"proj": A["even_in"], "out": A["even_out"]}, {"proj": A["odd_in"], "out": A["odd_out"]}]

        MHI = 2 * C + 2
        block = ctx.enter_context(nc.Block())

        @block.sync
        def _(sp):
            def load(t, src):
                if t.has(RAW):
                    sp.wait_ge(lo_done, t.count(1 - RAW))
                sp.dma_start(raw[:, t.slot, :], src).then_inc(raw_in[t.slot], 16)

            def load_all(src, first, count):
                with sp.Fori(0, count // RAW) as i:
                    for s in range(RAW):
                        load(Tile(first + s, i * RAW), src[i * RAW + s])

            sp.dma_start(cact, A["c"].broadcast_to([P, D])).then_inc(c_in, 16)

            def load_mod(q):
                if q >= 4:
                    sp.wait_ge(mod_used, 2 * (q - 3))
                sp.dma_start(modw[:, q % 4, :, :], A["w_mod"][q]).then_inc(mod_first_in[q % 4], 16)

            for q in range(4):
                load_mod(q)
            for dst, name in ((xT[:, :, :], "xT"), (norms[:, :, :, :], "norms"), (bmod[:, :, :], "bmod"),
                              (ident[:, :], "ident"), (ones[:, :], "ones"), (iota[:, :], "iota")):
                sp.dma_start(dst, A[name]).then_inc(const_in, 16)
            for l in range(LAYERS):
                b = base[l]
                proj, out = SRC[l]["proj"], SRC[l]["out"]
                if l == 0:
                    for q in range(4, MOD_FIRST):
                        load_mod(q)
                for s in range(RAW):
                    load(Tile(b["proj"] + s), proj[s])
                if l:
                    sp.wait_ge(x_ready, 16)
                mix = [(maskKQ, "maskKQ"), (negU, "negU"), (negones, "negones")] if l else [
                    (vg.rearrange("p a b -> p (a b)"), "v_gain"), (bs.rearrange("p a b -> p (a b)"), "b_s"),
                    (wsT, "wsT"), (gmask, "gmask"), (blk64, "blk64"), (rotM, "rotM"), (ropeC, "ropeC"),
                    (ropeS, "ropeS"), (maskQK, "maskQK"), (small[:, 0:2], "qk_gain")]
                for dst, name in mix:
                    src = A[name].broadcast_to([P, GM * P]) if name in ("v_gain", "b_s") else A[name]
                    sp.dma_start(dst, src).then_inc(mix_in, 16)
                sp.dma_start(subk, A["subkeys"][l]).then_inc(subk_in, 16)
                for s in range(RAW, EVEN_T if l == 0 else ODD_T):
                    load(Tile(b["proj"] + s), proj[s])
                load_all(out, b["out"], OUT_T)
                load_all(A["w_q"][l], b["wq"], WQ_T)
                load_all(A["u"][l], b["u"], NKEYS)
                load_all(A["v"][l], b["v"], NKEYS)
            sp.wait_ge(x_ready, 32)
            sp.dma_start(O["y"], xT[:, :, :]).then_inc(out_done, 16)
            sp.wait_ge(out_done, 16)

        MIX0, MIX1 = 16 * 10, 16 * 13
        CONSTS = 16 * 6

        @block.gpsimd
        def _(pool):
            def load_mod(q, dyn=0):
                pool.wait_ge(mod_used, 2 * (q - 3 + dyn))
                pool.dma_start(modw[:, q % 4, :, :], A["w_mod"][q + dyn]).then_inc(mod_in[q % 4], 16)

            body = Body(pool, pool_own)

            def pick_keys(l):
                shape = [P, TT, TOPK, TOPK]
                row = iota[:, 0:TOPK].unsqueeze(1).unsqueeze(1).broadcast_to(shape)
                with pool.Fori(0, HEADS) as i:
                    pool.wait_ge(picks_ready, HEADS * l + 1 + i)
                    for q, key in enumerate((keyI, keyJ)):
                        body.seq(pool.tensor_tensor(eq, row, places[:, :, q, :].unsqueeze(3).broadcast_to(shape),
                                                    ALU.subtract))
                        body.seq(pool.tensor_scalar(eq, eq, 0.0, None, ALU.is_equal))
                        body.seq(pool.tensor_tensor(eq, eq, keys[:, :, q, :].unsqueeze(2).broadcast_to(shape),
                                                    ALU.mult))
                        n = TOPK // 2
                        while n > 1:
                            body.seq(pool.tensor_tensor(eq[:, :, :, 0:n], eq[:, :, :, 0:n], eq[:, :, :, n:2 * n],
                                                        ALU.add))
                            n //= 2
                        body.seq(pool.tensor_tensor(picked, eq[:, :, :, 0], eq[:, :, :, 1], ALU.add))
                        ins = pool.tensor_copy(key[:, :, bass.ds(i, 1), :].squeeze(2), picked)
                        if q == 0:
                            body.seq(ins)
                        else:
                            ins.then_inc(keys_done, 1)
                    body.end()

            pool.wait_ge(const_in, CONSTS)
            pool.wait_ge(c_ready, 1)
            pool.tensor_copy(small[:, 48:49], ones[:, 0:1]).then_inc(keys_done, 1)
            pool.dma_start(kept_c, cact[0:1, :]).then_inc(c_kept, 16)
            with pool.Fori(0, (MOD_MIX + MOD_WQ) // 4) as i:
                for s in range(4):
                    load_mod(MOD_FIRST + s, 4 * i)
            pick_keys(0)
            pool.wait_ge(tile_done, base[0]["v"] + HALF)
            pool.wait_ge(c_kept, 16)
            pool.dma_start(cact, kept_c.broadcast_to([P, D])).then_inc(c_back, 16)
            with pool.Fori(0, (MOD_ALL - BEFORE_D) // 4) as i:
                for s in range(4):
                    load_mod(BEFORE_D + s, 4 * i)
            pick_keys(1)

        @block.scalar
        def _(act):
            own = Count()

            def hi(t):
                act.wait_ge(raw_in[t.slot], t.loaded())
                if t.has(2):
                    act.wait_ge(tile_done, t.count(-1))
                act.activation(whi[:, t.pair, :], raw[:, t.slot, :], ACT.Copy).then_inc(hi_done, 1)

            def evac(t, out, func=ACT.Copy, scale=1.0, h=None):
                act.wait_ge(tile_done, t.count(1))
                src = stream_bank(t)
                if h is not None:
                    src = bank[4 + t.slot][:, :].rearrange("p (a b) -> p a b", a=TT)[:, :, P * h:P * (h + 1)]
                act.activation(out, src, func, scale=scale).then_inc(act_evac, 1)

            def square(k, c):
                if k:
                    act.wait_ge(x_ready, 8 * (k - 1) + c + 1)
                act.activation(sq[:, c, :], xT[:, c, :], ACT.Square).then_inc(sq_ready, 1)

            def power(out, src, scale, done):
                act.activation(out, src, ACT.Ln, bias=eps[:, 0:1], scale=scale).then_inc(act_own, 1)
                act.wait_ge(act_own, own.add())
                act.activation(out, out, ACT.Exp, scale=-0.5).then_inc(done, 1)

            def norm(l, w):
                k, sh = 2 * l + w, 3 * C * w
                act.preload_act_table_set("natural_log_exp_and_others")
                for s in range(2):
                    hi(Tile(base[l]["wq" if w else "proj"] + s))
                act.wait_ge(ss_ready, k + 1)
                power(rs, norm_bank(k)[:, 0:T], 1.0 / D, rs_ready)
                for c in range(C):
                    act.wait_ge(h_ready, 8 * k + c + 1)
                    act.activation(mhi[:, c, :], hf[:, c, :], ACT.Identity,
                                   bias=modv[:, l, sh + c:sh + c + 1]).then_inc(mhi_ready, 1)

            act.preload_act_table_set("natural_log_exp_and_others")
            act.wait_ge(c_in, 16)
            act.activation(junk, cact, ACT.Exp, scale=-1.0).then_inc(act_own, 1)
            act.wait_ge(act_own, own.add())
            act.activation(junk, junk, ACT.Ln, bias=1.0).then_inc(act_own, 1)
            act.wait_ge(act_own, own.add())
            act.activation(junk, junk, ACT.Exp, scale=-1.0).then_inc(exp_c, 1)
            act.wait_ge(const_in, CONSTS)
            act.wait_ge(eps_ready, 1)
            for c in range(C):
                square(0, c)
            for l in range(LAYERS):
                b = base[l]
                if l:
                    for c in range(C):
                        square(2, c)
                norm(l, 0)
                pj = b["proj"]
                outs, first = [], 8 if l == 0 else 0
                pairs = 4 if l == 0 else 8
                for kind, k in projection_order(l):
                    if kind in ("ga", "va"):
                        outs.append([])
                    elif kind == "gb":
                        outs.append([(gv[:, :, 2 * k + h, :], ACT.Gelu_apprx_tanh, 1.0, h) for h in range(2)])
                    elif kind == "u":
                        outs.append([(uT[:, k, :], ACT.Gelu_apprx_tanh, 1.0, None)])
                    elif kind == "vb":
                        outs.append([(vbuf[:, k % 2, h, :, :], ACT.Copy, 1.0, h) for h in range(2)])
                    else:
                        to, r = (qk_raw if l == 0 else qk), "qk".index(kind)
                        outs.append([(to[:, k % 2, r, :], ACT.Copy, 0.125 if l and kind == "q" else 1.0, None)])
                def step(s, split=True, take=True):
                    if split and 2 <= s < len(outs):
                        hi(Tile(pj + s))
                    if take and 2 <= s < len(outs) + 2:
                        kind, k = projection_order(l)[s - 2]
                        done = k - 1 if kind in ("q", "k") else 2 * k - 2 if kind == "vb" else 0
                        if done > 0:
                            act.wait_ge(y_ready, 4 * l + done)
                        for out, func, scale, h in outs[s - 2]:
                            evac(Tile(pj + s - 2), out, func, scale, h)

                for s in range(first + AHEAD):
                    step(s)
                    if l == 0 and s == 6:
                        act.wait_ge(gvar, 1)
                        power(small[:, 16:24], small[:, 8:16], 1.0 / P, gsd)
                act.preload_act_table_set("natural_log_exp_and_others")
                def qk_norm(p):
                    act.wait_ge(act_evac, k_taken(0, p))
                    act.activation(sqqk, qk_raw[:, p % 2, :, :], ACT.Square).then_inc(qsq, 1)
                    act.wait_ge(qss, p + 1)
                    if p:
                        act.wait_ge(qn_ready, p)
                    power(rstd.rearrange("p a b -> p (a b)"), bank[3][:, :], 1.0 / HEAD, qsd)

                def softplus_log(p):
                    act.wait_ge(z_ready, 4 + p + 1)
                    for h in range(2):
                        ins = act.activation(pr[:, h, :], z_bank(p, h)[:, 0:384], ACT.Abs)
                    ins.then_inc(act_own, 1)
                    act.wait_ge(act_own, own.add())
                    act.activation(pr, pr, ACT.Exp, scale=-1.0).then_inc(act_own, 1)
                    act.wait_ge(act_own, own.add())
                    act.activation(pr, pr, ACT.Ln, bias=1.0).then_inc(z_ln, 1)

                if l == 0:
                    qk_norm(0)
                else:
                    step(first + AHEAD, take=False)
                    softplus_log(0)
                for p in range(pairs):
                    s, e = first + 3 * p + AHEAD, 4 * l + p + 1
                    step(s, split=l == 0)
                    if p == pairs - 1:
                        if l == 0:
                            act.wait_ge(ya_ready, 1)
                        act.wait_ge(y_ready, 4 * l + p)
                        act.wait_ge(tile_done, b["out"])
                        act.activation(mhi[:, 0:C - 1, :], yT[:, 0:C - 1, :], ACT.Copy).then_inc(mhi_ready, 1)
                    if l == 0:
                        step(s + 1)
                        act.wait_ge(s_sub, e)
                        act.activation(pr, st_, ACT.Exp, scale=0.125).then_inc(s_exp, 1)
                        step(s + 2)
                        if p + 1 < pairs:
                            qk_norm(p + 1)
                        for h in range(2):
                            act.wait_ge(pT_ready, 2 * p + h + 1)
                            act.activation(aT[:, h, :], bank[h][:, 0:384], ACT.Copy).then_inc(a_ready, 1)
                    else:
                        step(s + 1)
                        for h in range(2):
                            act.wait_ge(cum_ready, 2 * p + h + 1)
                            act.activation(aT[:, h, :], z_bank(p, h)[:, 0:384], ACT.Exp).then_inc(a_ready, 1)
                        step(s + 2)
                        step(s + 3, take=False)
                        if p + 1 < pairs:
                            softplus_log(p + 1)
                    act.wait_ge(yp_ready, e)
                    c = (GM if l == 0 else 0) + p
                    act.activation(yT[:, c, :], (z_bank(p, 0) if l else bank[0])[:, 0:T], ACT.Copy).then_inc(y_ready, 1)
                act.wait_ge(y_ready, 4 * l + pairs)
                act.activation(mhi[:, C - 1, :], yT[:, C - 1, :], ACT.Copy).then_inc(mhi_ready, 1)
                for s in range(OUT_T):
                    hi(Tile(b["out"] + s))
                    if s >= 4:
                        square(2 * l + 1, s - 4)
                for c in range(4, C):
                    square(2 * l + 1, c)
                norm(l, 1)

                def wq(s, dyn, lag=True):
                    if lag:
                        hi(Tile(b["wq"] + s, dyn))
                        evac(Tile(b["wq"] + s - 2, dyn), qT[:, s - 2 + dyn, :])
                for s in range(4):
                    wq(s, 0, s >= 2)
                with act.Fori(1, WQ_T // 4) as i:
                    for s in range(4):
                        wq(s, 4 * i)
                for s in range(WQ_T - 2, WQ_T):
                    evac(Tile(b["wq"] + s), qT[:, s, :])
                for h in range(HEADS):
                    act.wait_ge(sc_ready, HEADS * l + h + 1)
                    act.activation(scores[:, h, :, :, :].rearrange("p a b c -> p (a b c)"), bank[h % 4][:, :],
                                   ACT.Copy).then_inc(sc_used, 1)

                def u_step(s, dyn, lag=True):
                    hi(Tile(b["u"] + s, dyn))
                    if lag:
                        evac(Tile(b["u"] + s - 2, dyn), arena[:, bass.ds((s - 2) * T + dyn * T, T)],
                             ACT.Gelu_apprx_tanh)
                def next_head(h):
                    act.wait_ge(cur_used, HEADS * l + h)
                    act.activation(cur, scores[:, bass.ds(h, 1), :, :, :].squeeze(1), ACT.Copy).then_inc(cur_ready, 1)
                act.wait_ge(sc_used, HEADS * (l + 1))
                act.activation(cur, scores[:, 0, :, :, :], ACT.Copy).then_inc(cur_ready, 1)
                for s in range(8):
                    u_step(s, 0, s >= 2)
                with act.Fori(1, HALF // 8) as i:
                    for s in range(8):
                        if s == 0:
                            next_head(i)
                        u_step(s, 8 * i)
                act.wait_ge(best_ready, l + 1)
                act.activation(bestS, bestS, ACT.Exp).then_inc(bexp, 1)
                with act.Fori(HALF // 4, NKEYS // 4) as i:
                    for s in range(4):
                        u_step(s, 4 * i)
                for s in range(NKEYS - 2, NKEYS):
                    evac(Tile(b["u"] + s), arena[:, s * T:(s + 1) * T], ACT.Gelu_apprx_tanh)

                for half in range(2):
                    with act.Fori(half * HALF // 4, (half + 1) * HALF // 4) as i:
                        for s in range(4):
                            t = Tile(b["v"] + s, 4 * i)
                            if s == 0:
                                act.wait_ge(w_used, 128 * l + 64 * (half + 1))
                            act.wait_ge(tile_done, t.count(-1))
                            act.activation(ghi[:, t.pair, :], arena[:, bass.ds(s * T + i * (4 * T), T)],
                                           ACT.Copy).then_inc(ghi_done, 1)
                            hi(t)
                act.wait_ge(tile_done, b["v"] + NKEYS)
                for k in range(4):
                    act.activation(ysb[:, k // 2, 512 * (k % 2):512 * (k % 2) + 512], bank[4 + k][:, :],
                                   ACT.Copy).then_inc(y_copied, 1)

        @block.vector
        def _(dve):
            own = Count()

            def seq(ins):
                ins.then_inc(dve_own, 1)
                dve.wait_ge(dve_own, own.add())

            def lo(t):
                dve.wait_ge(hi_done, t.count(1))
                dve.tensor_tensor(wlo[:, t.pair, :], raw[:, t.slot, :], whi[:, t.pair, :].bitcast(f32),
                                  ALU.subtract).then_inc(lo_done, 1)

            def mod_rows(q, col, dyn=0, rows=(0, 1)):
                if q < MOD_FIRST:
                    dve.wait_ge(mod_first_in[q % 4], 16 * (q // 4 + 1))
                elif rows[0] == 0:
                    dve.wait_ge(mod_in[q % 4], 16 * ((q - MOD_FIRST) // 4 + 1) + 4 * dyn)
                for r in rows:
                    if q or r:
                        dve.wait_ge(mod_used, 2 * (q + dyn) + r)
                    dve.scalar_tensor_tensor(junk, modw[:, q % 4, r, :], 1.0, cact, ALU.mult, ALU.mult,
                                             accum_out=col[:, r:r + 1]).then_inc(mod_used, 1)

            def mod_add(a, b_, src):
                seq(dve.tensor_tensor(modv[:, :, :].rearrange("p a b -> p (a b)")[:, a:b_], src[:, a:b_],
                                      bmod[:, :, :].rearrange("p a b -> p (a b)")[:, a:b_], ALU.add))

            def mod_col(q):
                return modt[:, 2 * q:2 * q + 2]

            def norm(l, w):
                k, sh, sc = 2 * l + w, 3 * C * w, 3 * C * w + C
                seq(dve.scalar_tensor_tensor(gainA[:, :], modv[:, l, sc:sc + C], 1.0, norms[:, l, w, :], ALU.add,
                                             ALU.mult))
                for s in range(2):
                    lo(Tile(base[l]["wq" if w else "proj"] + s))
                if k == 0:
                    dve.tensor_copy(iota8[:, :, :], iota[:, :].unsqueeze(2).broadcast_to([P, NKEYS, STEP]))
                dve.wait_ge(rs_ready, k + 1)
                for half in range(2):
                    cs = range(4 * half, 4 * half + 4)
                    for c in cs:
                        dve.scalar_tensor_tensor(hf[:, c, :], xT[:, c, :], gainA[:, c:c + 1], rs, ALU.mult,
                                                 ALU.mult).then_inc(h_ready, 1)
                    for c in cs:
                        dve.wait_ge(mhi_ready, MHI * l + (C + 2) * w + c + 1)
                        ins = dve.scalar_tensor_tensor(mlo[:, c, :], hf[:, c, :], modv[:, l, sh + c:sh + c + 1],
                                                       mhi[:, c, :].bitcast(f32), ALU.add, ALU.subtract)
                    ins.then_inc(m_ready, 1)

            dve.wait_ge(exp_c, 1)
            dve.tensor_tensor(cact, cact, junk, ALU.mult).then_inc(c_ready, 1)
            dve.wait_ge(c_ready, 1)
            for q in range(MOD_FIRST):
                if q == 4:
                    dve.wait_ge(const_in, CONSTS)
                    dve.tensor_scalar(eps[:, :], ones[:, 0:1], EPS, None, ALU.mult).then_inc(eps_ready, 1)
                mod_rows(q, mod_col(q))
            dve.wait_ge(mod_used, 2 * MOD_FIRST)
            mod_add(0, 2 * C, modt)
            for l in range(LAYERS):
                b = base[l]
                norm(l, 0)
                pj = b["proj"]
                pairs = 4 if l == 0 else 8
                mods = list(range(MOD_FIRST, MOD_FIRST + MOD_MIX) if l == 0 else range(BEFORE_MIX1, MOD_ALL))

                def step(s):
                    if 2 <= s < (EVEN_T if l == 0 else ODD_T):
                        lo(Tile(pj + s))
                    if l == 0 and s < 8 + AHEAD and s in range(2, 13, 2):
                        mod_next()

                def mod_next():
                    if mods:
                        q = mods.pop(0)
                        mod_rows(q, mod_col(q))

                if l == 0:
                    dve.wait_ge(mix_in, MIX0)
                    seq(dve.tensor_tensor(wsT, wsT, gmask.unsqueeze(1).broadcast_to([P, GM, P]), ALU.mult))
                    for s in range(6):
                        step(s)
                    dve.wait_ge(act_evac, 4)
                    gvf = gv.rearrange("p a b c -> p (a b) c")
                    seq(dve.tensor_tensor(gsq, gvf, gvf, ALU.mult))
                    dve.tensor_reduce(small[:, 8:16], gsq, AX.X, ALU.add).then_inc(gvar, 1)
                    step(6)
                    step(7)
                    dve.wait_ge(gsd, 1)
                    seq(dve.tensor_tensor(vn.rearrange("p a b c -> p (a b) c"), gvf,
                                          small[:, 16:24].unsqueeze(2).broadcast_to([P, 8, P]), ALU.mult))
                    dve.tensor_tensor(vn, vn, vg.unsqueeze(1).broadcast_to([P, TT, GM, P]),
                                      ALU.mult).then_inc(vn_ready, 1)
                    step(8)
                    step(9)
                    dve.wait_ge(mixed, 1)
                    dve.wait_ge(act_evac, 8)
                    for g in range(GM):
                        m = bank[g // 2][:, T * (g % 2):T * (g % 2) + T].rearrange("p (a b) -> p a b", a=TT)
                        y = yT[:, g, :].rearrange("p (a b) -> p a b", a=TT)
                        seq(dve.tensor_tensor(y, m, bs[:, g, :].unsqueeze(1).broadcast_to([P, TT, P]), ALU.add))
                        ins = dve.tensor_tensor(yT[:, g, :], yT[:, g, :], uT[:, g, :], ALU.mult)
                    ins.then_inc(ya_ready, 1)
                    for s in range(10, 8 + AHEAD):
                        step(s)
                else:
                    for s in range(AHEAD):
                        step(s)
                def qk_norm(p):
                    dve.wait_ge(qsd, p + 1)
                    for r in range(2):
                        ins = dve.scalar_tensor_tensor(qn[:, r, :], qk_raw[:, p % 2, r, :], small[:, r:r + 1],
                                                       rstd[:, r, :], ALU.mult, ALU.mult)
                    ins.then_inc(qn_ready, 1)
                    dve.wait_ge(qn_ready, p + 1)
                    seq(dve.tensor_tensor(qk[:, p % 2, :, :], qn, ropeC.unsqueeze(1).broadcast_to([P, 2, T]),
                                          ALU.mult))
                    dve.wait_ge(qrot, p + 1)
                    seq(dve.tensor_tensor(rot, bank[2][:, :].rearrange("p (a b) -> p a b", a=2),
                                          ropeS.unsqueeze(1).broadcast_to([P, 2, T]), ALU.mult))
                    dve.tensor_tensor(qk[:, p % 2, :, :], qk[:, p % 2, :, :], rot, ALU.add).then_inc(qk_ready, 1)

                def split_y(n, cs):
                    dve.wait_ge(mhi_ready, MHI * l + C + 1 + n)
                    return dve.tensor_tensor(mlo[:, cs, :], yT[:, cs, :], mhi[:, cs, :].bitcast(f32), ALU.subtract)

                first = 8 if l == 0 else 0
                if l == 0:
                    qk_norm(0)
                for p in range(pairs):
                    s, e = first + 3 * p + AHEAD, 4 * l + p + 1
                    step(s)
                    if l == 0:
                        step(s + 1)
                        mx, rsum = small[:, 32:36], small[:, 36:40]
                        SEG = ((0, P), (P, 384))
                        dve.wait_ge(z_ready, e)
                        for h in range(2):
                            for k, (f, g) in enumerate(SEG):
                                seq(dve.tensor_reduce(mx[:, 2 * h + k:2 * h + k + 1], bank[h][:, f:g], AX.X, ALU.max))
                        for h in range(2):
                            for k, (f, g) in enumerate(SEG):
                                ins = dve.tensor_scalar(st_[:, h, f:g], bank[h][:, f:g],
                                                        mx[:, 2 * h + k:2 * h + k + 1], None, ALU.subtract)
                        ins.then_inc(s_sub, 1)
                        step(s + 2)
                        dve.wait_ge(s_exp, e)
                        for k, (f, g) in enumerate(SEG):
                            seq(dve.tensor_reduce(rsum[:, 2 * k:2 * k + 2], pr[:, :, f:g], AX.X, ALU.add))
                        seq(dve.reciprocal(rsum, rsum))
                        for h in range(2):
                            for k, (f, g) in enumerate(SEG):
                                ins = dve.tensor_scalar(pr[:, h, f:g], pr[:, h, f:g], rsum[:, 2 * k + h:2 * k + h + 1],
                                                        None, ALU.mult)
                        ins.then_inc(p_ready, 1)
                        if p + 1 < pairs:
                            qk_norm(p + 1)
                        mod_next()
                    else:
                        dve.wait_ge(z_ln, p + 1)
                        for h in range(2):
                            dve.scalar_tensor_tensor(st_[:, h, :], z_bank(p, h)[:, 0:384], 0.0, pr[:, h, :],
                                                     ALU.max, ALU.add).then_inc(sp_ready, 1)
                        step(s + 1)
                        step(s + 2)
                        mod_next()
                        mod_next()
                split_y(0, slice(0, C - 1))
                since, upto = (MOD_FIRST, MOD_FIRST + C // 2) if l == 0 else (BEFORE_MIX1, MOD_ALL)
                dve.wait_ge(mod_used, 2 * upto)
                mod_add(2 * since, 2 * upto, modt)
                split_y(1, slice(C - 1, C)).then_inc(m_ready, 1)
                for s in range(OUT_T + 2):
                    if s < OUT_T:
                        lo(Tile(b["out"] + s))
                    if s in (2, 4):
                        mod_next()
                    if s >= 2:
                        t, c = Tile(b["out"] + s - 2), s - 2
                        dve.wait_ge(tile_done, t.count(1))
                        dve.scalar_tensor_tensor(xT[:, c, :], stream_bank(t), modv[:, l, 2 * C + c:2 * C + c + 1],
                                                 xT[:, c, :], ALU.mult, ALU.add).then_inc(x_ready, 1)
                assert not mods
                if l == 0:
                    dve.wait_ge(mod_used, 2 * (MOD_FIRST + MOD_MIX))
                    mod_add(2 * upto, 2 * (MOD_FIRST + MOD_MIX), modt)
                norm(l, 1)
                if l == 0:
                    for s in range(2 * MOD_WQ):
                        if s >= 2:
                            lo(Tile(b["wq"] + s))
                        q = MOD_FIRST + MOD_MIX + s // 2
                        mod_rows(q, mod_col(q), rows=(s % 2,))
                    dve.wait_ge(mod_used, 2 * BEFORE_D)
                    mod_add(2 * (MOD_FIRST + MOD_MIX), 2 * BEFORE_D, modt)
                else:
                    lo(Tile(b["wq"] + 2))
                    lo(Tile(b["wq"] + 3))
                with dve.Fori(2 * MOD_WQ // 4 if l == 0 else 1, WQ_T // 4) as i:
                    for s in range(4):
                        lo(Tile(b["wq"] + s, 4 * i))

                body = Body(dve, dve_body)
                dve.wait_ge(sc_used, HEADS * (l + 1))
                with dve.Fori(0, HEADS) as i:
                    tiles = [Tile(b["u"] + s, 8 * i) for s in range(8)]

                    def lists(op, items, used=None):
                        n = len(items)
                        for k, item in enumerate(items):
                            body.wait(n - 1 if n <= body.n else 0)
                            ins = op(*item)
                            ins.then_inc(used, 1) if used is not None and k == n - 1 else body.go(ins)

                    def top8(c1, c2, top, idx):
                        return dve.max(top[:, 0:8], c1)

                    def drop8(c1, c2, top, idx):
                        return dve.match_replace(c2, top[:, 0:8], c1, -3e38)

                    def place8(c1, c2, top, idx):
                        return dve.max_index(idx[:, 0:8], top[:, 0:8], c1)

                    def next8(c1, c2, top, idx):
                        return dve.max(top[:, 8:16], c2)

                    def place16(c1, c2, top, idx):
                        return dve.max_index(idx[:, 8:16], top[:, 8:16], c2)

                    four = [(cur[:, a, q, :], cur2[:, a, q, :], v16[:, a, q, :], i16[:, a, q, :])
                            for a in range(TT) for q in range(2)]
                    two = [(cand[:, a, :, :].rearrange("p a b -> p (a b)"),
                            cand2[:, a, :, :].rearrange("p a b -> p (a b)"), best[:, a, :], pos[:, a, :])
                           for a in range(TT)]
                    dve.wait_ge(cur_ready, HEADS * l + 1 + i)
                    lo(tiles[0])
                    for item in four:
                        body.go(top8(*item))
                    lo(tiles[1])
                    lists(drop8, four)
                    lo(tiles[2])
                    for item in four:
                        ins = place8(*item)
                    ins.then_inc(cur_used, 1)
                    lo(tiles[3])
                    lists(next8, four)
                    lo(tiles[4])
                    lists(place16, four)
                    body.wait()
                    body.seq(dve.tensor_tensor(cand, v16[:, :, 0, :].unsqueeze(3).broadcast_to([P, TT, TOPK, TOPK]),
                                               v16[:, :, 1, :].unsqueeze(2).broadcast_to([P, TT, TOPK, TOPK]),
                                               ALU.add))
                    lo(tiles[5])
                    for item in two:
                        body.go(top8(*item))
                    lists(drop8, two)
                    lo(tiles[6])
                    for item in two:
                        place8(*item)
                    lists(next8, two)
                    lo(tiles[7])
                    lists(place16, two)
                    dve.wait_ge(keys_done, HEADS * l + 1 + i)
                    dve.tensor_copy(keys, i16)
                    body.wait()
                    body.go(dve.tensor_scalar(posA, pos, 4, None, ALU.logical_shift_right))
                    body.go(dve.tensor_scalar(posB, pos, TOPK - 1, None, ALU.bitwise_and))
                    body.go(dve.tensor_copy(bestS[:, :, bass.ds(i, 1), :].squeeze(2), best))
                    body.wait(1)
                    dve.tensor_copy(places[:, :, 0, :], posA)
                    dve.tensor_copy(places[:, :, 1, :], posB).then_inc(picks_ready, 1)
                    body.wait()
                    body.end()
                bshape = [P, TT, HEADS, TOPK]
                seq(dve.tensor_copy(ssum, bestS[:, :, :, 0]))
                dve.tensor_tensor(bestS, bestS, ssum.unsqueeze(3).broadcast_to(bshape),
                                  ALU.subtract).then_inc(best_ready, 1)
                dve.wait_ge(bexp, l + 1)
                seq(dve.tensor_reduce(ssum, bestS, AX.X, ALU.add))
                seq(dve.reciprocal(ssum, ssum))
                dve.tensor_tensor(bestS, bestS, ssum.unsqueeze(3).broadcast_to(bshape),
                                  ALU.mult).then_inc(gates_ready, 1)
                for s in range(5):
                    lo(Tile(b["u"] + HALF + s))
                dve.wait_ge(routeT, l + 1)
                seq(dve.tensor_copy(slotI[:, 0:T], bank[2][:, 0:T]))
                dve.tensor_copy(slotI[:, T:T + STEP], slotI[:, 0:STEP])
                dve.tensor_copy(route[:, 0, :], bank[2][:, T:2 * T])
                seq(dve.tensor_copy(route[:, 1, :], bank[3][:, 0:T]))
                seq(dve.tensor_tensor(rest, bank[3][:, 0:T], route[:, 1, :], ALU.subtract))
                seq(dve.tensor_copy(route[:, 2, :], rest))
                seq(dve.tensor_tensor(rest, rest, route[:, 2, :], ALU.subtract))
                seq(dve.tensor_copy(route[:, 3, :], rest))

                def first_keys(k, dyn=0):
                    if above(k, dyn, 2):
                        dve.wait_ge(w_done, 128 * l + 2 * (k - 1) + 2 * dyn)
                    t0 = STEP * (k if k <= STEPS else k - STEPS) + STEP * dyn
                    shape = [P, NKEYS, STEP]
                    dve.tensor_tensor(oneI[:, k % 2, :, :], iota8[:, :, :],
                                      slotI[:, bass.ds(t0, STEP)].unsqueeze(1).broadcast_to(shape),
                                      ALU.is_equal).then_inc(oneI_done, 1)

                def second_keys(k, dyn, half):
                    n = STEPS * (2 * l + half) + k
                    if above(n, dyn, 1):
                        dve.wait_ge(gJ_done, 3 * n + 3 * dyn)
                    shape = [P, HALF, STEP]
                    row = route[:, 0, bass.ds(STEP * k + STEP * dyn, STEP)].unsqueeze(1).broadcast_to(shape)
                    body.go(dve.tensor_tensor(isJ[:, :, :], iota8[:, HALF * half:HALF * (half + 1), :], row,
                                              ALU.is_equal))

                def gated(k, dyn, half):
                    n = STEPS * (2 * l + half) + k
                    body.wait()
                    if above(n, dyn, 2):
                        dve.wait_ge(w_done, 2 * (n - 1) + 2 * dyn)
                    for part in range(3):
                        g = route[:, 1 + part, bass.ds(STEP * k + STEP * dyn, STEP)]
                        dve.tensor_tensor(gJ[:, k % 2, part, :, :], isJ[:, :, :],
                                          g.unsqueeze(1).broadcast_to([P, HALF, STEP]), ALU.mult).then_inc(gJ_done, 1)

                def weigh(g, dyn, half):
                    total = l * 128 + 64 * half + g
                    dve.wait_ge(w_done, total + 1 + dyn)
                    t0 = g * GROUP + GROUP * dyn
                    part = arena[:, HALF * T * half:HALF * T * (half + 1)].rearrange("p (j t) -> p t j", t=T)
                    part = part[:, bass.ds(t0, GROUP), :]
                    w = bank[total % 2][:, 0:GROUP * HALF].rearrange("p (t j) -> p t j", t=GROUP)
                    dve.tensor_tensor(part, w, part, ALU.mult).then_inc(w_used, 1)

                def body_b(i, first=False, more=True):
                    for s in range(4):
                        if s % 2 == 0:
                            second_keys(s // 2, 2 * i, 0)
                        else:
                            first_keys((s + 1) // 2, 2 * i)
                        if more and not (first and s == 0):
                            lo(Tile(b["u"] + HALF + 4 + s, 4 * i))
                        if s % 2 == 0:
                            gated(s // 2, 2 * i, 0)
                        if first and s == 1:
                            dve.wait_ge(act_evac, acts[l]["u"] + HALF)
                        if not (first and s == 0):
                            weigh(s - 1, 4 * i, 0)
                    body.end()
                first_keys(0)
                body_b(0, first=True)
                with dve.Fori(1, 15) as i:
                    body_b(i)
                body_b(15, more=False)

                def g_lo(t, j):
                    dve.wait_ge(ghi_done, j + 1)
                    dve.tensor_tensor(glo[:, t.pair, :], arena[:, bass.ds((j - 128 * l) * T, T)],
                                      ghi[:, t.pair, :].bitcast(f32), ALU.subtract).then_inc(glo_done, 1)

                def body_c(i, first):
                    for s in range(4):
                        t = Tile(b["v"] + s, 4 * i)
                        if first and s == 0:
                            weigh(63, 0, 0)
                        if s % 2 == 0:
                            second_keys(s // 2, 2 * i, 1)
                        else:
                            first_keys(STEPS + (s + 1) // 2, 2 * i)
                        g_lo(t, 128 * l + s + 4 * i)
                        lo(t)
                        if s % 2 == 0:
                            gated(s // 2, 2 * i, 1)
                        if first and s == 1:
                            dve.wait_ge(act_evac, acts[l]["u"] + NKEYS)
                        if not (first and s == 0):
                            weigh(s - 1, 4 * i, 1)
                    body.end()
                body_c(0, True)
                with dve.Fori(1, 16) as i:
                    body_c(i, False)
                weigh(63, 0, 1)

                def body_d(dyn, between=lambda s: None):
                    for s in range(16):
                        t = Tile(b["v"] + HALF + s, dyn)
                        g_lo(t, 128 * l + HALF + s + dyn)
                        lo(t)
                        between(s)

                if l == 0:
                    dve.wait_ge(c_back, 16)
                with_mods = MOD_D // 4 if l == 0 else 0
                if l == 0:
                    with dve.Fori(0, with_mods) as i:
                        body_d(16 * i, lambda s: s % 2 or mod_rows(
                            BEFORE_D + s // 4, modt8[:, 2 * (s // 4):2 * (s // 4) + 2], 4 * i, ((s // 2) % 2,)))
                        dve.wait_ge(mod_used, 2 * BEFORE_D + 8 + 8 * i)
                        body.seq(dve.tensor_copy(modt[:, bass.ds(2 * BEFORE_D + 8 * i, 8)], modt8[:, :]))
                        body.end()
                    mod_add(2 * BEFORE_D, 2 * BEFORE_MIX1, modt)
                with dve.Fori(with_mods, HALF // 16) as i:
                    body_d(16 * i)
                for c in range(C):
                    if c % 2 == 0:
                        dve.wait_ge(yT_ready, 4 * l + c // 2 + 1)
                    dve.scalar_tensor_tensor(xT[:, c, :], bank[c // 2][:, T * (c % 2):T * (c % 2) + T],
                                             modv[:, l, 5 * C + c:5 * C + c + 1], xT[:, c, :], ALU.mult,
                                             ALU.add).then_inc(x_ready, 1)

        @block.tensor
        def _(pe):

            def weights(t, halves=None):
                out = stream_bank(t)
                pe.wait_ge(hi_done, t.count(1))
                for c in range(C):
                    w = whi[:, t.pair, c * P:(c + 1) * P]
                    if halves is not None and c % (C // 2) == 0:
                        pe.wait_ge(m_ready, halves + c // (C // 2))
                    pe.matmul(out, w, mhi[:, c, :], start=c == 0, stop=False)
                    pe.matmul(out, w, mlo[:, c, :], start=False, stop=False)
                pe.wait_ge(lo_done, t.count(1))
                for c in range(C):
                    ins = pe.matmul(out, wlo[:, t.pair, c * P:(c + 1) * P], mhi[:, c, :], start=False,
                                    stop=c == C - 1)
                ins.then_inc(tile_done, 1)

            def wide_weights(t, half):
                out = bank[4 + (t.slot + 1 - half) % RAW]
                pe.wait_ge(hi_done, t.count(1))
                for a in range(TT):
                    o, ms = out[:, 2 * P * a:2 * P * (a + 1)], slice(a * P, (a + 1) * P)
                    for c in range(C // 2):
                        w, k = whi[:, t.pair, 2 * P * c:2 * P * (c + 1)], C // 2 * half + c
                        pe.matmul(o, mhi[:, k, ms], w, start=a == 0 and k == 0, stop=False, skip_group_check=True)
                        pe.matmul(o, mlo[:, k, ms], w, start=False, stop=False, skip_group_check=True)
                pe.wait_ge(lo_done, t.count(1))
                for a in range(TT):
                    o, ms = out[:, 2 * P * a:2 * P * (a + 1)], slice(a * P, (a + 1) * P)
                    for c in range(C // 2):
                        ins = pe.matmul(o, mhi[:, C // 2 * half + c, ms], wlo[:, t.pair, 2 * P * c:2 * P * (c + 1)],
                                        start=False, stop=half == 1 and c == C // 2 - 1, skip_group_check=True)
                ins.then_inc(tile_done, 1)

            def sum_square(k, c):
                pe.wait_ge(sq_ready, 8 * k + max(c + 1, 2))
                ins = pe.matmul(norm_bank(k)[:, 0:T], ones[:, :], sq[:, c, :], start=c == 0, stop=c == C - 1)
                if c == C - 1:
                    ins.then_inc(ss_ready, 1)

            pe.wait_ge(const_in, CONSTS)
            for l in range(LAYERS):
                b = base[l]
                for c in range(C):
                    sum_square(2 * l, c)
                pj, ae = b["proj"], acts[l]["proj"]
                if l:
                    pe.wait_ge(y_copied, 4)
                tiles = EVEN_T if l == 0 else ODD_T
                first = 8 if l == 0 else 0
                pairs = 4 if l == 0 else 8

                def step(s):
                    if s >= tiles:
                        return
                    kind = projection_order(l)[s][0]
                    next_bank = kind in ("ga", "va")
                    if s + next_bank >= 4:
                        pe.wait_ge(act_evac, ae + s + next_bank - 3)
                    if kind in ("ga", "gb", "va", "vb"):
                        if s < 2:
                            pe.wait_ge(m_ready, 5 * l + s + 1)
                        wide_weights(Tile(pj + s), int(kind[1] == "b"))
                    else:
                        weights(Tile(pj + s))

                for s in range(first + AHEAD):
                    step(s)
                    if l == 0 and s == 9:
                        pe.wait_ge(vn_ready, 1)
                        for g in range(GM):
                            for a in range(TT):
                                at = T * (g % 2) + a * P
                                ins = pe.matmul(bank[g // 2][:, at:at + P], vn[:, a, g, :], wsT[:, g, :],
                                                start=True, stop=True)
                        ins.then_inc(mixed, 1)
                pe.wait_ge(mix_in, MIX1 if l else MIX0)
                def qk_sums(p):
                    pe.wait_ge(qsq, p + 1)
                    if p:
                        pe.wait_ge(qsd, p)
                    for r in range(2):
                        ins = pe.matmul(bank[3][:, r * T:(r + 1) * T], blk64, sqqk[:, r, :], start=True, stop=True)
                    ins.then_inc(qss, 1)

                def qk_rotated(p):
                    pe.wait_ge(qn_ready, p + 1)
                    if p:
                        pe.wait_ge(qk_ready, p)
                    for r in range(2):
                        ins = pe.matmul(bank[2][:, r * T:(r + 1) * T], rotM, qn[:, r, :], start=True, stop=True)
                    ins.then_inc(qrot, 1)

                def key_query(p):
                    pe.wait_ge(act_evac, k_taken(1, p))
                    if p >= 2:
                        pe.wait_ge(y_ready, 4 + p - 1)
                    for h in range(2):
                        z, hd = z_bank(p, h), slice(HEAD * h, HEAD * (h + 1))
                        q, k = qk[:, p % 2, 0, :], qk[:, p % 2, 1, :]
                        pe.matmul(z[:, 0:T], k[hd, 0:P], q[hd, :], start=True, stop=False, skip_group_check=True)
                        pe.matmul(z[:, 0:P], ident[:, :], maskKQ, start=False, stop=False, skip_group_check=True)
                        pe.matmul(z[:, T:384], k[hd, P:T], q[hd, P:T], start=False, stop=False,
                                  skip_group_check=True)
                        ins = pe.matmul(z[:, T:384], ident[:, :], maskKQ, start=False, stop=True,
                                        skip_group_check=True)
                    ins.then_inc(z_ready, 1)

                if l == 0:
                    qk_sums(0)
                    qk_rotated(0)
                else:
                    key_query(0)
                for p in range(pairs):
                    s, e = first + 3 * p + AHEAD, 4 * l + p + 1
                    q, k, v = qk[:, p % 2, 0, :], qk[:, p % 2, 1, :], vbuf[:, (p // 2) % 2, p % 2, :, :]
                    heads = [slice(HEAD * h, HEAD * (h + 1)) for h in range(2)]
                    step(s)
                    if l == 0:
                        pe.wait_ge(qk_ready, p + 1)
                        if p == 0:
                            pe.wait_ge(ya_ready, 1)
                        else:
                            pe.wait_ge(a_ready, 2 * p)
                            pe.wait_ge(y_ready, p)
                        for h, hd in enumerate(heads):
                            z = bank[h]
                            pe.matmul(z[:, 0:P], q[hd, 0:P], k[hd, 0:P], start=True, stop=False,
                                      skip_group_check=True)
                            pe.matmul(z[:, 0:P], ident[:, :], maskQK, start=False, stop=False,
                                      skip_group_check=True)
                            pe.matmul(z[:, P:384], q[hd, P:T], k[hd, :], start=False, stop=False,
                                      skip_group_check=True)
                            ins = pe.matmul(z[:, T:384], ident[:, :], maskQK, start=False, stop=True,
                                            skip_group_check=True)
                        ins.then_inc(z_ready, 1)
                        step(s + 1)
                        step(s + 2)
                        if p + 1 < pairs:
                            qk_sums(p + 1)
                        pe.wait_ge(p_ready, p + 1)
                        for h in range(2):
                            for r in range(3):
                                ins = pe.transpose(bank[h][:, r * P:(r + 1) * P], pr[:, h, r * P:(r + 1) * P],
                                                   ident[:, :])
                            ins.then_inc(pT_ready, 1)
                        if p + 1 < pairs:
                            qk_rotated(p + 1)
                    else:
                        for h in range(2):
                            z, sp_ = z_bank(p, h), st_[:, h, :]
                            pe.wait_ge(sp_ready, 2 * p + h + 1)
                            pe.matmul(z[:, 0:T], negU, sp_[:, 0:T], start=False, stop=False, skip_group_check=True)
                            pe.matmul(z[:, P:T], negones, sp_[:, T:384], start=False, stop=False,
                                      skip_group_check=True)
                            pe.matmul(z[:, T:384], negU, sp_[:, T:384], start=False, stop=True,
                                      skip_group_check=True).then_inc(cum_ready, 1)
                        step(s + 1)
                        step(s + 2)
                        if p + 1 < pairs:
                            key_query(p + 1)
                    pe.wait_ge(y_ready, e - 1) if e > 1 else None
                    for h, hd in enumerate(heads):
                        pe.wait_ge(a_ready, 2 * (e - 1) + h + 1)
                        yo = z_bank(p, 0) if l else bank[0]
                        pe.matmul(yo[hd, 0:T], v[:, 0, hd], aT[:, h, 0:T], start=True, stop=False,
                                  skip_group_check=True)
                        ins = pe.matmul(yo[hd, P:T], v[:, 1, hd], aT[:, h, T:384], start=False, stop=True,
                                        skip_group_check=True)
                    ins.then_inc(yp_ready, 1)

                pe.wait_ge(m_ready, 5 * l + 3)
                for s in range(OUT_T):
                    if s >= 4:
                        pe.wait_ge(x_ready, 16 * l + s - 3)
                    weights(Tile(b["out"] + s))
                    if s >= 6:
                        sum_square(2 * l + 1, 2 * (s - 6))
                        sum_square(2 * l + 1, 2 * (s - 6) + 1)
                for c in range(4, C):
                    sum_square(2 * l + 1, c)

                def ring(name, s, dyn, halves=None):
                    pe.wait_ge(act_evac, acts[l][name] + s - 3 + dyn)
                    weights(Tile(b[name] + s, dyn), halves)

                for s in range(4):
                    ring("wq", s, 0, None if s else 5 * l + 4)
                with pe.Fori(1, WQ_T // 4) as i:
                    for s in range(4):
                        ring("wq", s, 4 * i)
                pe.wait_ge(act_evac, acts[l]["u"])
                pe.wait_ge(subk_in, 16 * (l + 1))
                for h in range(HEADS):
                    if h >= 4:
                        pe.wait_ge(sc_used, HEADS * l + h - 3)
                    for a in range(TT):
                        for q in range(2):
                            r = (2 * a + q) * P
                            ins = pe.matmul(bank[h % 4][:, r:r + P], qT[:, 2 * h + q, a * P:(a + 1) * P],
                                            subk[:, 2 * h + q, :], start=True, stop=True)
                    ins.then_inc(sc_ready, 1)
                with pe.Fori(0, HALF // 4) as i:
                    for s in range(4):
                        ring("u", s, 4 * i)
                for s in range(4):
                    ring("u", HALF + s, 0)
                pe.wait_ge(keys_done, HEADS * (l + 1) + 1)
                for a in range(TT):
                    for src, at in ((keyI, 0), (keyJ, T)):
                        pe.transpose(bank[2][:, at + a * P:at + (a + 1) * P],
                                     src[:, a, :, :].rearrange("p a b -> p (a b)"), ident[:, :])
                pe.wait_ge(gates_ready, l + 1)
                for a in range(TT):
                    ins = pe.transpose(bank[3][:, a * P:(a + 1) * P], bestS[:, a, :, :].rearrange("p a b -> p (a b)"),
                                       ident[:, :])
                ins.then_inc(routeT, 1)

                def onehot_product(g, dyn, half, half_dyn=0):
                    total = l * 128 + 64 * half + g
                    if g % 2 == 0:
                        k = STEPS * half + g // 2
                        pe.wait_ge(oneI_done, (2 * STEPS + 1) * l + k + 1 + half_dyn)
                        pe.wait_ge(gJ_done, 3 * (2 * STEPS * l + k + 1) + 3 * half_dyn)
                    if above(total, dyn, 2):
                        pe.wait_ge(w_used, total - 1 + dyn)
                    two = (g // 2) % 2
                    for k in range(GROUP):
                        out, at = bank[total % 2][:, HALF * k:HALF * (k + 1)], GROUP * (g % 2) + k
                        for part in range(3):
                            ins = pe.matmul(out, oneI[:, two, :, at], gJ[:, two, part, :, at],
                                            start=part == 0, stop=part == 2)
                    ins.then_inc(w_done, 1)

                def body_b(i, more=True):
                    for s in range(4):
                        if more:
                            ring("u", HALF + 4 + s, 4 * i)
                        onehot_product(s, 4 * i, 0, 2 * i)
                body_b(0)
                with pe.Fori(1, 15) as i:
                    body_b(i)
                body_b(15, more=False)

                def v_tile(s, dyn, start=False, stop=False):
                    t = Tile(b["v"] + s, dyn)
                    vs = [slice(512 * h, 512 * h + 512) for h in range(2)]
                    ts_ = [slice(a * P, (a + 1) * P) for a in range(TT)]
                    pe.wait_ge(hi_done, t.count(1))
                    pe.wait_ge(ghi_done, 128 * l + s + 1 + dyn)
                    for a in range(TT):
                        for h in range(2):
                            pe.matmul(bank[4 + 2 * a + h][:, :], ghi[:, t.pair, ts_[a]], whi[:, t.pair, vs[h]],
                                      start=start, stop=False, skip_group_check=True)
                    pe.wait_ge(glo_done, 128 * l + s + 1 + dyn)
                    for a in range(TT):
                        for h in range(2):
                            pe.matmul(bank[4 + 2 * a + h][:, :], glo[:, t.pair, ts_[a]], whi[:, t.pair, vs[h]],
                                      start=False, stop=False, skip_group_check=True)
                    pe.wait_ge(lo_done, t.count(1))
                    for a in range(TT):
                        for h in range(2):
                            ins = pe.matmul(bank[4 + 2 * a + h][:, :], ghi[:, t.pair, ts_[a]],
                                            wlo[:, t.pair, vs[h]], start=False, stop=stop, skip_group_check=True)
                    return ins.then_inc(tile_done, 1)

                def body_c(i, start):
                    for s in range(4):
                        v_tile(s, 4 * i, start and s == 0)
                        onehot_product(s, 4 * i, 1, 2 * i)
                pe.wait_ge(act_evac, acts[l]["u"] + NKEYS)
                body_c(0, True)
                with pe.Fori(1, 16) as i:
                    body_c(i, False)
                with pe.Fori(16, 31) as i:
                    for s in range(4):
                        v_tile(s, 4 * i)
                for s in range(4):
                    ins = v_tile(NKEYS - 4 + s, 0, False, s == 3)
                for c in range(C):
                    for a in range(TT):
                        if c == 0:
                            pe.wait_ge(y_copied, 4 * l + 2 * a + 1)
                            pe.wait_ge(w_used, 128 * (l + 1))
                        if c == 4:
                            pe.wait_ge(y_copied, 4 * l + 2 * a + 2)
                        at = T * (c % 2) + a * P
                        ins = pe.transpose(bank[c // 2][:, at:at + P], ysb[:, a, c * P:(c + 1) * P], ident[:, :])
                    if c % 2:
                        ins.then_inc(yT_ready, 1)


def constants():
    f = np.float32
    r = np.arange(P)
    q = r % HEAD
    ident = np.eye(P, dtype=f)
    inv = (500000.0 ** (-np.arange(ROPE_HALF, dtype=f) / ROPE_HALF)).astype(f)
    ang = np.arange(T, dtype=f)[None, :] * inv[q % ROPE_HALF][:, None]
    roped = (q < 2 * ROPE_HALF)[:, None]
    rot = np.zeros((P, P), f)
    for m in r:
        if q[m] < ROPE_HALF:
            rot[m + ROPE_HALF, m] = -1
        elif q[m] < 2 * ROPE_HALF:
            rot[m - ROPE_HALF, m] = 1
    return {
        "ident": ident, "ones": np.ones((P, P), f), "iota": np.tile(r.astype(f), (P, 1)),
        "blk64": (r[:, None] // HEAD == r[None, :] // HEAD).astype(f), "rotM": rot,
        "ropeC": np.where(roped, np.cos(ang), 1).astype(f), "ropeS": np.where(roped, np.sin(ang), 0).astype(f),
        "negU": -(r[:, None] >= r[None, :]).astype(f), "negones": -np.ones((P, P), f),
        "maskKQ": np.where(r[:, None] >= r[None, :], NEG, 0).astype(f),
        "maskQK": np.where(r[None, :] > r[:, None], NEG, 0).astype(f),
        "gmask": (r[:, None] <= r[None, :]).astype(f),
    }


def kernel(**inputs):
    import concourse.bacc as bacc
    from concourse.bass_utils import run_bass_kernel_spmd

    x = {k: np.asarray(v) for k, v in inputs.items()}
    pack = np.ascontiguousarray

    def tiles(w):
        return pack(w.reshape(C, P, -1, P).transpose(2, 1, 0, 3)).reshape(-1, P, D)

    def ordered(w, l, starts):
        out = []
        for kind, k in projection_order(l):
            if kind in ("ga", "gb", "va", "vb"):
                at = starts[kind[0]] + 2 * P * k
                half = w[D // 2 * (kind[1] == "b"):, at:at + 2 * P][:D // 2]
                out.append(half.reshape(C // 2, P, 2 * P).transpose(1, 0, 2).reshape(P, D))
            else:
                at = starts[kind] + P * k
                out.append(tiles(w[:, at:at + P])[0])
        return np.stack(out)

    gw = GM * P
    even = ordered(x["even_w_in"][0], 0, {"g": gw, "u": 0, "q": 2 * gw, "k": 3 * gw, "v": 4 * gw})
    odd = ordered(x["odd_w_in"][0], 1, {"q": 0, "k": D, "v": 2 * D})
    gains = np.stack([np.concatenate([x[n][0]] * 2) for n in ("moba_q_gain", "moba_k_gain")], axis=1)
    data = {
        "xT": pack(x["x"][0].T.reshape(C, P, T).transpose(1, 0, 2)), "c": x["c"],
        "w_mod": pack(x["w_mod"].transpose(0, 2, 1).reshape(MOD_ALL, 2, P, D).transpose(0, 2, 1, 3)),
        "bmod": pack(x["b_mod"].reshape(LAYERS, MODC, P).transpose(2, 0, 1)),
        "norms": pack(np.stack([x["norm_mix"], x["norm_ffn"]], 1).reshape(LAYERS, 2, C, P).transpose(3, 0, 1, 2)),
        "even_in": even, "even_out": tiles(x["even_w_out"][0]),
        "odd_in": odd, "odd_out": tiles(x["odd_w_out"][0]),
        "w_q": np.stack([tiles(w) for w in x["peer_w_q"]]),
        "subkeys": pack(x["peer_subkeys"].transpose(0, 4, 1, 2, 3)).reshape(LAYERS, P, 2 * HEADS, P),
        "u": np.stack([pack(u.reshape(P, P, C, P).transpose(1, 3, 2, 0)).reshape(NKEYS, P, D)
                       for u in x["peer_u"]]),
        "v": np.stack([pack(v.reshape(P, P, D).transpose(1, 0, 2)) for v in x["peer_v"]]),
        "v_gain": x["gmlp_v_gain"].reshape(1, gw), "b_s": x["gmlp_b_s"].reshape(1, gw),
        "wsT": pack(x["gmlp_w_s"][0].transpose(2, 0, 1)), "qk_gain": pack(gains),
    }
    data.update(constants())
    nc = bacc.Bacc("TRN2", target_bir_lowering=False, num_devices=1)
    A = {n: nc.dram_tensor(f"in_{n}", a.shape, mybir.dt.float32, kind="ExternalInput").ap() for n, a in data.items()}
    O = {"y": nc.dram_tensor("out_y", (P, C, T), mybir.dt.float32, kind="ExternalOutput").ap()}
    program(nc, A, O)
    r = run_bass_kernel_spmd(nc, [{f"in_{n}": a for n, a in data.items()}], core_ids=[0])
    y = r.results[0]["out_y"]
    return pack(y.transpose(2, 1, 0)).reshape(1, T, D)
```
